# Optimizing a Trainium2 kernel written in Bass

```python
import math
import jax, jax.numpy as jnp
from jax import lax
import numpy as np

D_MODEL = 1024
BATCH = 1
SEQ = 256
DEPTH = 2

D_FF = 2816
GDN_HEADS = 4
GDN_HEAD_DIM = 128
GDN_CONV = 4
GDN_CHUNK = 64
GDN_KEY = GDN_HEADS * GDN_HEAD_DIM
GDN_VAL = GDN_HEADS * GDN_HEAD_DIM
SC_GROUPS = 4
SC_CHANNELS = 512
SC_CONV = 3
HYB_IN = 2 * GDN_KEY + 2 * GDN_VAL + 2 * GDN_HEADS + 3 * SC_CHANNELS
HYB_MIX = GDN_VAL + SC_CHANNELS
SWA_HEADS = 16
SWA_KV_HEADS = 4
SWA_HEAD_DIM = 64
SWA_WINDOW = 128
SWA_QKV = (SWA_HEADS + 2 * SWA_KV_HEADS) * SWA_HEAD_DIM
SWA_OUT = SWA_HEADS * SWA_HEAD_DIM
ROPE_THETA = 10000.0
RMS_EPS = 1e-6
L2_EPS = 1e-6

kernel_name = "hybrid_gdn_shortconv_swa_macaron"

def rmsnorm(x, g):
    xf = x.astype(jnp.float32)
    y = xf * lax.rsqrt(jnp.mean(xf * xf, axis=-1, keepdims=True) + RMS_EPS)
    return (y * g.astype(jnp.float32)).astype(x.dtype)

def swiglu(x, w_gate, w_up, w_down):
    return (jax.nn.silu(x @ w_gate) * (x @ w_up)) @ w_down

def causal_dwconv(x, w):
    width, ch = w.shape
    return lax.conv_general_dilated(
        x, w[:, None, :].astype(x.dtype), window_strides=(1,), padding=[(width - 1, 0)],
        dimension_numbers=("NWC", "WIO", "NWC"), feature_group_count=ch)

def l2norm(x):
    return x * lax.rsqrt(jnp.sum(x * x, axis=-1, keepdims=True) + L2_EPS)

def gated_delta_chunked(q, k, v, beta, g):
    b_, t_, h_, dk = q.shape
    dv = v.shape[-1]
    c_ = GDN_CHUNK
    n_ = t_ // c_

    def to_chunks(a):
        a = a.reshape((b_, n_, c_, h_) + a.shape[3:])
        return jnp.moveaxis(a, 3, 1)

    q, k, v, beta, g = (to_chunks(a) for a in (q, k, v, beta, g))
    q = q * (dk ** -0.5)
    g_cum = jnp.cumsum(g, axis=-1)
    idx = jnp.arange(c_)
    lower_incl = idx[:, None] >= idx[None, :]
    decay = jnp.exp(jnp.where(lower_incl, g_cum[..., :, None] - g_cum[..., None, :], -jnp.inf))
    k_beta = k * beta[..., None]
    v_beta = v * beta[..., None]
    m = jnp.einsum("bhncd,bhnsd->bhncs", k_beta, k) * decay
    rhs = jnp.concatenate([v_beta, k_beta * jnp.exp(g_cum)[..., None]], axis=-1)
    sol = lax.linalg.triangular_solve(m, rhs, left_side=True, lower=True, unit_diagonal=True)
    u, w = sol[..., :dv], sol[..., dv:]
    attn_intra = jnp.einsum("bhncd,bhnsd->bhncs", q, k) * decay
    q_g = q * jnp.exp(g_cum)[..., None]
    g_last = g_cum[..., -1]
    k_g = k * jnp.exp(g_last[..., None] - g_cum)[..., None]
    xs = tuple(jnp.moveaxis(a, 2, 0) for a in (q_g, w, u, attn_intra, k_g, jnp.exp(g_last)))

    def step(state, inp):
        qg, wc, uc, a, kg, dl = inp
        v_new = uc - jnp.einsum("bhcd,bhde->bhce", wc, state)
        o = jnp.einsum("bhcd,bhde->bhce", qg, state) + jnp.einsum("bhcs,bhse->bhce", a, v_new)
        state = state * dl[..., None, None] + jnp.einsum("bhcd,bhce->bhde", kg, v_new)
        return state, o

    s0 = jnp.zeros((b_, h_, dk, dv), jnp.float32)
    _, o = lax.scan(step, s0, xs)
    o = jnp.moveaxis(jnp.moveaxis(o, 0, 2), 1, 3)
    return o.reshape(b_, t_, h_, dv)

def hybrid_gdn_shortconv(h, w_in, gdn_conv_w, a_log, dt_bias, out_norm, sc_conv_w, w_out):
    b_, t_, _ = h.shape
    p = h @ w_in
    sizes = [GDN_KEY, GDN_KEY, GDN_VAL, GDN_VAL, GDN_HEADS, GDN_HEADS,
             SC_CHANNELS, SC_CHANNELS, SC_CHANNELS]
    q, k, v, z, b_raw, a_raw, sc_b, sc_c, sc_h = jnp.split(p, np.cumsum(sizes)[:-1].tolist(), axis=-1)
    qkv = jax.nn.silu(causal_dwconv(jnp.concatenate([q, k, v], axis=-1), gdn_conv_w)).astype(jnp.float32)
    q, k, v = jnp.split(qkv, [GDN_KEY, 2 * GDN_KEY], axis=-1)
    q = l2norm(q.reshape(b_, t_, GDN_HEADS, GDN_HEAD_DIM))
    k = l2norm(k.reshape(b_, t_, GDN_HEADS, GDN_HEAD_DIM))
    v = v.reshape(b_, t_, GDN_HEADS, GDN_HEAD_DIM)
    beta = jax.nn.sigmoid(b_raw.astype(jnp.float32))
    g = -jnp.exp(a_log.astype(jnp.float32)) * jax.nn.softplus(
        a_raw.astype(jnp.float32) + dt_bias.astype(jnp.float32))
    o = gated_delta_chunked(q, k, v, beta, g)
    o = o * lax.rsqrt(jnp.mean(o * o, axis=-1, keepdims=True) + RMS_EPS)
    zf = z.astype(jnp.float32).reshape(b_, t_, GDN_HEADS, GDN_HEAD_DIM)
    o = (o * out_norm.astype(jnp.float32) * jax.nn.silu(zf)).reshape(b_, t_, GDN_VAL).astype(h.dtype)
    y_sc = sc_b * causal_dwconv(sc_c * sc_h, sc_conv_w)
    return jnp.concatenate([o, y_sc], axis=-1) @ w_out

def rope(x, pos):
    half = x.shape[-1] // 2
    inv = ROPE_THETA ** (-jnp.arange(half, dtype=jnp.float32) / half)
    ang = pos.astype(jnp.float32)[:, None] * inv[None, :]
    cos, sin = jnp.cos(ang)[None, :, None, :], jnp.sin(ang)[None, :, None, :]
    xf = x.astype(jnp.float32)
    x1, x2 = xf[..., :half], xf[..., half:]
    return jnp.concatenate([x1 * cos - x2 * sin, x2 * cos + x1 * sin], axis=-1).astype(x.dtype)

def sliding_window_attention(h, w_qkv, b_qkv, sinks, w_o, b_o):
    b_, t_, _ = h.shape
    grp = SWA_HEADS // SWA_KV_HEADS
    win = SWA_WINDOW
    nb = t_ // win
    d = SWA_HEAD_DIM
    qkv = h @ w_qkv + b_qkv
    q, k, v = jnp.split(qkv, [SWA_HEADS * d, (SWA_HEADS + SWA_KV_HEADS) * d], axis=-1)
    pos = jnp.arange(t_)
    q = rope(q.reshape(b_, t_, SWA_HEADS, d), pos)
    k = rope(k.reshape(b_, t_, SWA_KV_HEADS, d), pos)
    v = v.reshape(b_, t_, SWA_KV_HEADS, d)
    qb = q.reshape(b_, nb, win, SWA_KV_HEADS, grp, d)

    def band(a):
        ap = jnp.pad(a, ((0, 0), (win, 0), (0, 0), (0, 0))).reshape(b_, nb + 1, win, SWA_KV_HEADS, d)
        return jnp.concatenate([ap[:, :-1], ap[:, 1:]], axis=2)

    kb, vb = band(k), band(v)
    s = jnp.einsum("bnqhgd,bnkhd->bnhgqk", qb, kb, preferred_element_type=jnp.float32) * (d ** -0.5)
    qi = jnp.arange(win)[:, None]
    kj = jnp.arange(2 * win)[None, :]
    in_window = (kj > qi) & (kj <= qi + win)
    valid = in_window[None] & ((jnp.arange(nb)[:, None, None] > 0) | (kj[None] >= win))
    s = jnp.where(valid[None, :, None, None], s, -jnp.inf)
    sink = sinks.astype(jnp.float32).reshape(1, 1, SWA_KV_HEADS, grp, 1, 1)
    mx = jnp.maximum(jnp.max(s, axis=-1, keepdims=True), sink)
    e = jnp.exp(s - mx)
    p = e / (jnp.sum(e, axis=-1, keepdims=True) + jnp.exp(sink - mx))
    o = jnp.einsum("bnhgqk,bnkhd->bnqhgd", p.astype(vb.dtype), vb)
    return o.reshape(b_, t_, SWA_OUT) @ w_o + b_o

def setup_inputs(seed: int = 0) -> dict:
    key = jax.random.key(seed)
    ks = iter(jax.random.split(key, 40))
    f32 = jnp.float32

    def nrm(shape, scale):
        return scale * jax.random.normal(next(ks), shape, f32)

    ne, no = (DEPTH + 1) // 2, DEPTH // 2
    D, F = D_MODEL, D_FF
    x = nrm((BATCH, SEQ, D), 1.0)
    ffn1_norm = 1.0 + nrm((DEPTH, D), 0.02)
    ffn1_w_gate = nrm((DEPTH, D, F), D ** -0.5)
    ffn1_w_up = nrm((DEPTH, D, F), D ** -0.5)
    ffn1_w_down = nrm((DEPTH, F, D), F ** -0.5)
    mix_norm = 1.0 + nrm((DEPTH, D), 0.02)
    ffn2_norm = 1.0 + nrm((DEPTH, D), 0.02)
    ffn2_w_gate = nrm((DEPTH, D, F), D ** -0.5)
    ffn2_w_up = nrm((DEPTH, D, F), D ** -0.5)
    ffn2_w_down = nrm((DEPTH, F, D), F ** -0.5)
    hyb_w_in = nrm((ne, D, HYB_IN), D ** -0.5)
    gdn_conv_w = nrm((ne, GDN_CONV, 2 * GDN_KEY + GDN_VAL), GDN_CONV ** -0.5)
    gdn_a_log = jnp.log(jax.random.uniform(next(ks), (ne, GDN_HEADS), f32, 1.0, 16.0))
    dt = jnp.exp(jax.random.uniform(next(ks), (ne, GDN_HEADS), f32, math.log(1e-3), math.log(1e-1)))
    gdn_dt_bias = dt + jnp.log(-jnp.expm1(-dt))
    gdn_out_norm = 1.0 + nrm((ne, GDN_HEAD_DIM), 0.02)
    sc_conv_w = nrm((ne, SC_CONV, SC_CHANNELS), SC_CONV ** -0.5)
    hyb_w_out = nrm((ne, HYB_MIX, D), HYB_MIX ** -0.5)
    swa_w_qkv = nrm((no, D, SWA_QKV), D ** -0.5)
    swa_b_qkv = nrm((no, SWA_QKV), 0.02)
    swa_sinks = nrm((no, SWA_HEADS), 0.5)
    swa_w_o = nrm((no, SWA_OUT, D), SWA_OUT ** -0.5)
    swa_b_o = nrm((no, D), 0.02)
    final_norm = 1.0 + nrm((D,), 0.02)
    return {"x": x,
            "ffn1_norm": ffn1_norm, "ffn1_w_gate": ffn1_w_gate, "ffn1_w_up": ffn1_w_up, "ffn1_w_down": ffn1_w_down,
            "mix_norm": mix_norm,
            "ffn2_norm": ffn2_norm, "ffn2_w_gate": ffn2_w_gate, "ffn2_w_up": ffn2_w_up, "ffn2_w_down": ffn2_w_down,
            "hyb_w_in": hyb_w_in, "gdn_conv_w": gdn_conv_w, "gdn_a_log": gdn_a_log, "gdn_dt_bias": gdn_dt_bias,
            "gdn_out_norm": gdn_out_norm, "sc_conv_w": sc_conv_w, "hyb_w_out": hyb_w_out,
            "swa_w_qkv": swa_w_qkv, "swa_b_qkv": swa_b_qkv, "swa_sinks": swa_sinks, "swa_w_o": swa_w_o,
            "swa_b_o": swa_b_o, "final_norm": final_norm}

def reference(x, ffn1_norm, ffn1_w_gate, ffn1_w_up, ffn1_w_down, mix_norm,
              ffn2_norm, ffn2_w_gate, ffn2_w_up, ffn2_w_down,
              hyb_w_in, gdn_conv_w, gdn_a_log, gdn_dt_bias, gdn_out_norm, sc_conv_w, hyb_w_out,
              swa_w_qkv, swa_b_qkv, swa_sinks, swa_w_o, swa_b_o, final_norm):
    for li in range(DEPTH):
        x = x + 0.5 * swiglu(rmsnorm(x, ffn1_norm[li]), ffn1_w_gate[li], ffn1_w_up[li], ffn1_w_down[li])
        h = rmsnorm(x, mix_norm[li])
        j = li // 2
        if li % 2 == 0:
            x = x + hybrid_gdn_shortconv(h, hyb_w_in[j], gdn_conv_w[j], gdn_a_log[j], gdn_dt_bias[j],
                                         gdn_out_norm[j], sc_conv_w[j], hyb_w_out[j])
        else:
            x = x + sliding_window_attention(h, swa_w_qkv[j], swa_b_qkv[j], swa_sinks[j],
                                             swa_w_o[j], swa_b_o[j])
        x = x + 0.5 * swiglu(rmsnorm(x, ffn2_norm[li]), ffn2_w_gate[li], ffn2_w_up[li], ffn2_w_down[li])
    return rmsnorm(x, final_norm)


_drawn_inputs = setup_inputs


def setup_inputs(seed=0):
    import zlib

    import numpy as np

    out = dict(_drawn_inputs(seed))
    spreads = {}
    factors = {'ffn1_norm': 4.058,
     'ffn2_norm': 6.202,
     'gdn_out_norm': 28.078,
     'swa_b_qkv': 28.816,
     'swa_sinks': 64.0,
     'swa_b_o': 30.112,
     'final_norm': 7.978,
     'swa_w_qkv': 4.078,
     'swa_w_o': 3.971}
    for name, (base, spread) in spreads.items():
        noise = np.random.default_rng([zlib.crc32(name.encode()), seed]).standard_normal(out[name].shape)
        drawn = base * np.exp(spread * noise) if base else spread * noise
        out[name] = __import__('jax').numpy.asarray(drawn.astype(out[name].dtype))
    for name, factor in factors.items():
        out[name] = (out[name] * factor).astype(out[name].dtype)
    return out
```

```python
from contextlib import ExitStack

import concourse.bass as bass
from concourse import mybir

ALU = mybir.AluOpType
ACT = mybir.ActivationFunctionType
F32 = mybir.dt.float32
F32R = mybir.dt.float32r
BF16 = mybir.dt.bfloat16
AX = mybir.AxisListType

P = 128
RING = 3
CW = 256
MASKED = -1.0e30

K_IDENT = 0
K_TRI = 128
K_BLK = 256
K_LEVEL = 384
N_LEVEL = 6
K_ATT0 = K_LEVEL + N_LEVEL * 128
K_ATT1 = K_ATT0 + 128
K_COS = K_ATT1 + 256
K_SIN = K_COS + 128
K_END = K_SIN + 128


def constants():
    import numpy as np

    t = np.zeros((P, K_END), np.float32)
    s = np.arange(P)[:, None]
    c = np.arange(P)[None, :]
    same = (s // 64) == (c // 64)
    t[:, K_IDENT:K_IDENT + 128] = s == c
    t[:, K_TRI:K_TRI + 128] = same & (s <= c)
    t[:, K_BLK:K_BLK + 128] = same
    for n in range(N_LEVEL):
        b = 1 << n
        t[:, K_LEVEL + 128 * n:K_LEVEL + 128 * (n + 1)] = (
            (s // (2 * b) == c // (2 * b)) & (s % (2 * b) < b) & (c % (2 * b) >= b))
    t[:, K_ATT0:K_ATT0 + 128] = np.where(c <= s, 0.0, MASKED)
    kj = np.arange(256)[None, :]
    t[:, K_ATT1:K_ATT1 + 256] = np.where((kj > s) & (kj <= s + 128), 0.0, MASKED)
    half = 32
    inv = (np.float32(10000.0) ** (-np.arange(half, dtype=np.float32) / np.float32(half))).astype(np.float32)
    ang = np.arange(256, dtype=np.float32)[:, None] * inv[None, :]
    cos, sin = np.cos(ang), np.sin(ang)
    for b in range(2):
        rows = slice(128 * b, 128 * b + 128)
        t[:, K_COS + 64 * b:K_COS + 64 * b + 64] = np.concatenate([cos[rows], cos[rows]], 1)
        t[:, K_SIN + 64 * b:K_SIN + 64 * b + 64] = np.concatenate([-sin[rows], sin[rows]], 1)
    return t


def trunk(nc, t, out, mix=(True, True)):
    SEQ, D = t["x"].shape[1:]
    DEPTH, _, FF = t["ffn1_w_gate"].shape
    KT = D // P
    PAIRS = KT // 2
    TB = SEQ // P
    NG = FF // CW
    HG = CW // P
    FFN_CHUNKS = 3 * NG
    EPS = 1e-6
    assert (SEQ, D, DEPTH) == (256, 1024, 2) and FF == NG * CW

    HYB_IN, HYB_OUT = 14, D // CW
    SWA_IN, SWA_OUT = 6, D // CW
    first = {}
    at = 0
    for name, n, use in (("ffn0", FFN_CHUNKS, 1), ("hyb_in", HYB_IN, mix[0]), ("hyb_out", HYB_OUT, mix[0]),
                         ("ffn1", FFN_CHUNKS, 1), ("ffn2", FFN_CHUNKS, 1), ("swa_in", SWA_IN, mix[1]),
                         ("swa_out", SWA_OUT, mix[1]), ("ffn3", FFN_CHUNKS, 1)):
        first[name] = at
        at += n if use else 0
    CHUNKS = at
    ffn_w = [("ffn1", 0), ("ffn2", 0), ("ffn1", 1), ("ffn2", 1)]

    with ExitStack() as ctx:
        def sb(name, shape, dt=F32):
            return ctx.enter_context(nc.sbuf_tensor(name, shape, dt))

        def sem(name):
            return ctx.enter_context(nc.semaphore(name))

        raw = sb("raw", [P, RING, 2048])
        w_hi = [sb(f"w_hi{n}", [P, 2048], F32R) for n in range(RING)]
        w_lo = [sb(f"w_lo{n}", [P, 2048], F32R) for n in range(RING)]
        kon = sb("kon", [P, K_END])
        ident = kon[:, K_IDENT:K_IDENT + P]
        ones = sb("ones", [P, P])
        zeros = sb("zeros", [P, P], BF16)
        xT = sb("xT", [P, KT, SEQ])
        h_hi = sb("h_hi", [P, KT, SEQ], F32R)
        h_lo = sb("h_lo", [P, KT, SEQ], F32R)
        m_hi = sb("m_hi", [P, KT, SEQ], F32R)
        m_lo = sb("m_lo", [P, KT, SEQ], F32R)
        sq = sb("sq", [P, PAIRS, 2 * SEQ])
        var = sb("var", [P, SEQ + TB])
        rstd = sb("rstd", [P, SEQ + TB])
        neg_half = sb("neg_half", [P, 1])
        gate = sb("gate", [P, 2 * SEQ])
        silu = sb("silu", [P, 2 * SEQ])
        silu_r = sb("silu_r", [P, 2 * SEQ])
        act = sb("act", [P, 2 * SEQ])
        act_hi = sb("act_hi", [P, 2, SEQ], F32R)
        act_lo = sb("act_lo", [P, 2, SEQ], F32R)
        NVEC = 7 * KT + 48 + 12 + 1
        vecT = sb("vecT", [P, NVEC])
        V_NORM, V_CONV, V_SC, V_GN, V_BO = 0, 6 * KT, 6 * KT + 48, 6 * KT + 60, 6 * KT + 61
        work = sb("work", [P, 16 * 1024])
        rstd_half = work[:, 15 * 1024:15 * 1024 + SEQ]
        vec_rows = work[0:NVEC, 14 * 1024:14 * 1024 + P]

        fin_ss = sb("fin_ss", [P, TB, 2])
        fin_v = sb("fin_v", [P, TB])
        fin_r = sb("fin_r", [P, TB])
        bank = [ctx.enter_context(nc.psum_tensor(f"bank{n}", [P, 512], F32)) for n in range(8)]
        GATE, UP, ACC, AUX, AUX2 = bank[0], bank[1], bank[2:6], bank[6], bank[7]
        OUT_BANKS = [GATE, UP, AUX, AUX2]

        w_loaded = [sem(f"w_loaded{n}") for n in range(RING)]
        hi_split = sem("hi_split")
        lo_split = sem("lo_split")
        w_used = sem("w_used")
        final_loaded = sem("final_loaded")
        x_loaded = sem("x_loaded")
        x_loaded2 = sem("x_loaded2")
        rest_loaded = sem("rest_loaded")
        vec_loaded = sem("vec_loaded")
        small_loaded = sem("small_loaded")
        set_up = sem("set_up")
        vec_tr = sem("vec_tr")
        vec_ready = sem("vec_ready")
        acc_done = sem("acc_done")
        x_updated = sem("x_updated")
        sq_ready = sem("sq_ready")
        sq_summed = sem("sq_summed")
        sq_step = sem("sq_step")
        ss_ready = sem("ss_ready")
        var_ready = sem("var_ready")
        rstd_ready = sem("rstd_ready")
        h_hi_ready = sem("h_hi_ready")
        h_ready = sem("h_ready")
        gate_read = sem("gate_read")
        silu_ready = sem("silu_ready")
        silu_r_ready = sem("silu_r_ready")
        up_read = sem("up_read")
        act_hi_ready = sem("act_hi_ready")
        act_ready = sem("act_ready")
        rstd_step = sem("rstd_step")
        half_ready = sem("half_ready")
        fin_acc = sem("fin_acc")
        fin_dve = sem("fin_dve")
        fin_sq = sem("fin_sq")
        fin_rstd = sem("fin_rstd")
        fin_step = sem("fin_step")
        out_ready = sem("out_ready")
        stored = sem("stored")

        def number(ch):
            return ch[0] + RING * ch[1]

        def slot(ch):
            return ch[0] % RING

        def load(sp, ch, src, check=True):
            if check:
                sp.wait_ge(lo_split, number(ch) - RING + 1)
            n = src.shape[1]
            sp.dma_start(raw[:, slot(ch), :].rearrange("p (a b) -> p a b", a=n), src) \
              .then_inc(w_loaded[slot(ch)], 16)

        def split_hi(act_e, ch, check=True):
            act_e.wait_ge(w_loaded[slot(ch)], 16 * (ch[0] // RING + 1 + ch[1]))
            if check:
                act_e.wait_ge(w_used, number(ch) - RING + 1)
            nc.scalar.activation(w_hi[slot(ch)][:], raw[:, slot(ch), :], ACT.Copy).then_inc(hi_split, 1)

        def split_lo(eng, ch, by=nc.vector, handed_over=False):
            eng.wait_ge(hi_split, number(ch) + 1)
            if handed_over:
                eng.wait_ge(lo_split, number(ch))
            by.tensor_tensor(w_lo[slot(ch)][:], raw[:, slot(ch), :], w_hi[slot(ch)][:].bitcast(F32),
                                    ALU.subtract).then_inc(lo_split, 1)

        def product(out_ap, s, wcols, mv_hi, mv_lo, start, stop=False):
            nc.tensor.matmul(out_ap, w_hi[s][:, wcols], mv_hi, start=start, stop=False, skip_group_check=True)
            nc.tensor.matmul(out_ap, w_hi[s][:, wcols], mv_lo, start=False, stop=False, skip_group_check=True)
            return nc.tensor.matmul(out_ap, w_lo[s][:, wcols], mv_hi, start=False, stop=stop,
                                    skip_group_check=True)

        def column_chunk(pe, ch, dst, m_hi, m_lo, pairs_ready=None, between=None):
            pe.wait_ge(lo_split, number(ch) + 1)
            order = [(kt, ft) for kt in range(KT) for ft in range(HG)]
            if pairs_ready is None:
                order = [(kt, ft) for ft in range(HG) for kt in range(KT)]
            for n, (kt, ft) in enumerate(order):
                if pairs_ready is not None and kt % 2 == 0 and ft == 0:
                    pe.wait_ge(pairs_ready[0], pairs_ready[1] + kt // 2 + 1)
                if between is not None and n == KT:
                    between()
                last = product(dst[:, ft * SEQ:(ft + 1) * SEQ], slot(ch),
                               slice(kt * CW + ft * P, kt * CW + (ft + 1) * P),
                               m_hi[:, kt, :], m_lo[:, kt, :], start=(n == 0), stop=(kt == KT - 1))
            last.then_inc(w_used, 1)

        def norm_ss(pe, n):
            pe.wait_ge(sq_summed, n + 1)
            if n:
                pe.wait_ge(var_ready, n)
            for half in range(2):
                nc.tensor.matmul(AUX[:, 0:SEQ], ones[:], sq[:, 0, half * SEQ:(half + 1) * SEQ],
                                 start=(half == 0), stop=(half == 1))
            for b in range(TB):
                for half in range(2):
                    o = half * SEQ + b * P
                    last = nc.tensor.matmul(AUX[:, SEQ + b:SEQ + b + 1], sq[:, 0, o:o + P], ones[:, 0:1],
                                            start=(half == 0), stop=(half == 1))
            last.then_inc(ss_ready, 1)

        def norm_scalar(act_e, n, before_pair=None):
            for j in range(PAIRS):
                if before_pair is not None:
                    before_pair(j)
                act_e.wait_ge(x_updated, PAIRS * n + j + 1)
                if n:
                    act_e.wait_ge(sq_summed, n)
                    act_e.wait_ge(ss_ready, n)
                for kt in (2 * j, 2 * j + 1):
                    g = V_NORM + KT * n + kt
                    i = nc.scalar.activation(h_hi[:, kt, :], xT[:, kt, :], ACT.Copy, scale=vecT[:, g:g + 1])
                i.then_inc(h_hi_ready, 1)
                nc.scalar.activation(sq[:, j, :], xT[:, 2 * j:2 * j + 2, :].rearrange("p a b -> p (a b)"),
                                     ACT.Square).then_inc(sq_ready, 1)

        def norm_lo(dve, n, j):
            dve.wait_ge(h_hi_ready, PAIRS * n + j + 1)
            for kt in (2 * j, 2 * j + 1):
                g = V_NORM + KT * n + kt
                i = nc.vector.scalar_tensor_tensor(out=h_lo[:, kt, :], in0=xT[:, kt, :], scalar=vecT[:, g:g + 1],
                                                   in1=h_hi[:, kt, :].bitcast(F32), op0=ALU.mult,
                                                   op1=ALU.subtract)
            i.then_inc(h_ready, 1)

        def norm_vector(dve, n, banks, ready, bias=None, after_pair=None):
            for j in range(PAIRS):
                dve.wait_ge(*ready[j])
                pair = xT[:, 2 * j:2 * j + 2, :].rearrange("p a b -> p (a b)")
                if n == 0:
                    nc.vector.tensor_copy(pair, banks[j][:]).then_inc(x_updated, 1)
                elif bias is None:
                    nc.vector.tensor_tensor(pair, banks[j][:], pair, ALU.add).then_inc(x_updated, 1)
                else:
                    for kt in (2 * j, 2 * j + 1):
                        i = nc.vector.scalar_tensor_tensor(
                            out=xT[:, kt, :], in0=banks[j][:, (kt % 2) * SEQ:(kt % 2 + 1) * SEQ],
                            scalar=bias[:, kt:kt + 1], in1=xT[:, kt, :], op0=ALU.add, op1=ALU.add)
                    i.then_inc(x_updated, 1)
                if after_pair is not None and j == 0:
                    after_pair(0)
                if j:
                    norm_lo(dve, n, j - 1)
                if after_pair is not None and j == 2:
                    after_pair(1)
            norm_lo(dve, n, PAIRS - 1)
            if after_pair is not None:
                after_pair(2)

        def norm_pool(pool, n):
            for j in range(1, PAIRS):
                pool.wait_ge(sq_ready, PAIRS * n + j + 1)
                if j > 1:
                    pool.wait_ge(sq_step, 2 * n + j - 1)
                i = nc.gpsimd.tensor_tensor(sq[:, 0, :], sq[:, 0, :], sq[:, j, :], ALU.add)
                i.then_inc(sq_step if j < PAIRS - 1 else sq_summed, 1)


        def norm_var(dve, n):
            dve.wait_ge(ss_ready, n + 1)
            nc.vector.tensor_scalar(var[:], AUX[:, 0:SEQ + TB], 1.0 / D, EPS, ALU.mult, ALU.add) \
              .then_inc(rstd_step, 1)
            dve.wait_ge(rstd_step, n + 1)
            nc.vector.reciprocal(var[:], var[:]).then_inc(var_ready, 1)

        def norm_rstd(act_e, n):
            act_e.wait_ge(var_ready, n + 1)
            nc.scalar.activation(rstd[:], var[:], ACT.Sqrt).then_inc(rstd_ready, 1)

        def norm_half(pool, n):
            pool.wait_ge(rstd_ready, n + 1)
            nc.gpsimd.tensor_scalar(rstd_half[:], rstd[:, 0:SEQ], 0.5, None, ALU.mult).then_inc(half_ready, 1)
            pool.wait_ge(half_ready, halves_before(n) + 1)

        def halves_before(n):
            return sum(kind == "ffn" for kind, f in stages[:n])

        def over_rows(row, tiles):
            return row.rearrange("p (a s) -> p a s", a=1).to_broadcast([P, tiles, SEQ])

        def ffn_sources(f):
            kind, li = ffn_w[f]
            wg = t[kind + "_w_gate"][li].rearrange("(k p) f -> p k f", p=P)
            wu = t[kind + "_w_up"][li].rearrange("(k p) f -> p k f", p=P)
            wd = t[kind + "_w_down"][li].rearrange("(g k p) d -> g p k d", p=P, k=HG)
            return wg, wu, wd

        def ffn_sync(sp, f):
            c0 = first[f"ffn{f}"]
            wg, wu, wd = ffn_sources(f)
            load(sp, (c0, 0), wg[:, :, 0:CW], check=c0 >= RING)
            load(sp, (c0 + 1, 0), wu[:, :, 0:CW], check=c0 >= RING)

            def group(i):
                cols = bass.ds((i + 1) * CW, CW)
                load(sp, (c0 + 2, i), wg[:, :, cols], check=not isinstance(i, int) or i > 0 or c0 >= RING)
                load(sp, (c0 + 3, i), wu[:, :, cols])
                load(sp, (c0 + 4, i), wd[i])

            group(0)
            with sp.Fori(1, NG - 1) as i:
                group(i)
            load(sp, (c0 + FFN_CHUNKS - 1, 0), wd[NG - 1])

        def ffn_scalar(act_e, f, n):
            c0 = first[f"ffn{f}"]

            def gate_step(g):
                act_e.wait_ge(gate_read, NG * f + g + 1)
                if not isinstance(g, int) or g + f:
                    act_e.wait_ge(silu_r_ready, NG * f + g)
                nc.scalar.activation(silu[:], gate[:], ACT.Silu).then_inc(silu_ready, 1)

            def next_split(ch, last_group=False):
                if not last_group or ch[0] + RING * (ch[1] + 1) < CHUNKS:
                    split_hi(act_e, (ch[0] + RING, ch[1]))

            def act_step(g):
                act_e.wait_ge(up_read, NG * f + g + 1)
                nc.scalar.activation(act_hi[:].rearrange("p a b -> p (a b)"), act[:], ACT.Copy) \
                  .then_inc(act_hi_ready, 1)

            gate_step(0)
            next_split((c0, 0))
            next_split((c0 + 1, 0))
            act_step(0)

            def group(i, last_group):
                gate_step(i + 1)
                next_split((c0 + 2, i), last_group)
                next_split((c0 + 3, i), last_group)
                act_e.wait_ge(w_used, number((c0 + 4, i)) + 1)
                act_step(i + 1)
                next_split((c0 + 4, i), last_group)

            with act_e.Fori(0, NG - 2) as i:
                group(i, False)
            group(NG - 2, True)

        def ffn_vector(dve, f, n):
            c0 = first[f"ffn{f}"]

            def gate_step(g, ch):
                dve.wait_ge(w_used, number(ch) + 1)
                if not isinstance(g, int) or g + f:
                    dve.wait_ge(silu_ready, NG * f + g)
                nc.vector.tensor_tensor(gate[:].rearrange("p (a s) -> p a s", a=2),
                                        GATE[:].rearrange("p (a s) -> p a s", a=2),
                                        over_rows(rstd[:, 0:SEQ], 2), ALU.mult).then_inc(gate_read, 1)

            def up_step(g, ch):
                dve.wait_ge(w_used, number(ch) + 1)
                dve.wait_ge(silu_r_ready, NG * f + g + 1)
                nc.vector.tensor_tensor(act[:], UP[:], silu_r[:], ALU.mult).then_inc(up_read, 1)

            def lo_step(g):
                dve.wait_ge(act_hi_ready, NG * f + g + 1)
                nc.vector.tensor_tensor(act_lo[:].rearrange("p a b -> p (a b)"), act[:],
                                        act_hi[:].rearrange("p a b -> p (a b)").bitcast(F32),
                                        ALU.subtract).then_inc(act_ready, 1)

            def next_split(ch, last_group=False):
                if not last_group or ch[0] + RING * (ch[1] + 1) < CHUNKS:
                    split_lo(dve, (ch[0] + RING, ch[1]))

            gate_step(0, (c0, 0))
            next_split((c0, 0))
            up_step(0, (c0 + 1, 0))
            next_split((c0 + 1, 0))
            lo_step(0)

            def group(i, last_group):
                gate_step(i + 1, (c0 + 2, i))
                next_split((c0 + 2, i), last_group)
                up_step(i + 1, (c0 + 3, i))
                next_split((c0 + 3, i), last_group)
                lo_step(i + 1)
                next_split((c0 + 4, i), last_group)

            with dve.Fori(0, NG - 2) as i:
                group(i, False)
            group(NG - 2, True)

        def ffn_pool(pool, f):
            with pool.Fori(0, NG) as g:
                pool.wait_ge(silu_ready, g + (NG * f + 1))
                nc.gpsimd.tensor_tensor(silu_r[:].rearrange("p (a s) -> p a s", a=2),
                                        silu[:].rearrange("p (a s) -> p a s", a=2),
                                        over_rows(rstd_half[:], 2), ALU.mult).then_inc(silu_r_ready, 1)

        def ffn_tensor(pe, f, n):
            c0 = first[f"ffn{f}"]
            final = f == 3

            def gate_chunk(g, ch, pairs_ready=None):
                column_chunk(pe, ch, GATE, h_hi, h_lo, pairs_ready)

            def down_chunk(ch, g, done=None):
                pe.wait_ge(lo_split, number(ch) + 1)
                pe.wait_ge(act_ready, NG * f + g + 1)
                s = slot(ch)
                if final:
                    for b in range(TB):
                        for half in range(2):
                            for k in range(HG):
                                tok = slice(b * P, (b + 1) * P)
                                cols = slice(k * D + half * 512, k * D + (half + 1) * 512)
                                o = ACC[2 * b + half][:]
                                for st, mv in ((act_hi, w_hi), (act_lo, w_hi), (act_hi, w_lo)):
                                    last = nc.tensor.matmul(o, st[:, k, tok], mv[s][:, cols], start=False,
                                                            stop=False, skip_group_check=True)
                        if done is not None and b < TB - 1:
                            last.then_inc(done, 1)
                else:
                    for dt in range(KT):
                        for k in range(HG):
                            last = product(ACC[dt // 2][:, (dt % 2) * SEQ:(dt % 2 + 1) * SEQ], s,
                                           slice(k * D + dt * P, k * D + (dt + 1) * P),
                                           act_hi[:, k, :], act_lo[:, k, :], start=False)
                        if done is not None and dt % 2 and dt < KT - 1:
                            last.then_inc(done, 1)
                last.then_inc(w_used, 1)

            gate_chunk(0, (c0, 0), (h_ready, PAIRS * n))
            norm_ss(pe, n)
            column_chunk(pe, (c0 + 1, 0), UP, h_hi, h_lo)
            if final:
                for b in range(TB):
                    for kt in range(KT):
                        nc.tensor.matmul(ACC[2 * b + kt // 4][:, (kt % 4) * P:(kt % 4 + 1) * P],
                                         xT[:, kt, b * P:(b + 1) * P], ident, start=(kt % 4 == 0), stop=False,
                                         skip_group_check=True)
            else:
                for j in range(PAIRS):
                    nc.tensor.matmul(ACC[j][:], zeros[:],
                                     zeros[:].rearrange("p (a s) -> p a s", a=1).to_broadcast([P, 4, P]), start=True, stop=False,
                                     skip_group_check=True)

            def group(i):
                pe.wait_ge(gate_read, i + (NG * f + 1))
                gate_chunk(None, (c0 + 2, i))
                pe.wait_ge(up_read, i + (NG * f + 1))
                column_chunk(pe, (c0 + 3, i), UP, h_hi, h_lo)
                down_chunk((c0 + 4, i), i)

            with pe.Fori(0, NG - 1) as i:
                group(i)
            down_chunk((c0 + FFN_CHUNKS - 1, 0), NG - 1, done=fin_acc if final else acc_done)

        fin_t = work[:, 2048:4096]
        final_g = work[:, 4096:4096 + D]
        x_in = work[:, 0:TB * D].rearrange("p (b d) -> p b d", b=TB)
        y_out = work[:, 0:TB * D].rearrange("p (b d) -> p b d", b=TB)

        KEY = 512
        HEADS = 4
        DK = KEY // HEADS
        SCC = 4 * KEY + 2 * HEADS
        HYB_COLS = [KEY, KEY + CW, 0, CW, SCC + 512, SCC + 512 + CW, 2 * KEY, 2 * KEY + CW, SCC + 1024,
                    SCC + 1024 + CW, SCC, SCC + CW, 3 * KEY, 3 * KEY + CW]
        KINDS = "kqcvhbz"
        CHUNK = 64
        JC = P // CHUNK
        NS = TB * HEADS

        def room(k, n=1):
            return work[:, k * 1024:(k + n) * 1024]

        def by_tile(ap):
            return ap.rearrange("p (h s) -> p h s", s=SEQ)

        def by_pair(ap, b):
            return ap.rearrange("p (b h s) -> p b h s", b=TB, h=HEADS)[:, b]

        def one(ap, b, h):
            n = b * HEADS + h
            return ap[:, n * P:(n + 1) * P]

        def bank_pair(bk):
            return bk[:].rearrange("p (h s) -> p h s", h=HEADS)

        def spread(cols, b):
            return cols[:, b * HEADS:(b + 1) * HEADS].rearrange("p (h s) -> p h s", s=1) \
                .to_broadcast([P, HEADS, P])

        def wide(cols):
            return cols.rearrange("p (n s) -> p n s", s=1).to_broadcast([P, NS, P])

        def table(col, n):
            return kon[:, col:col + P].rearrange("p (a s) -> p a s", a=1).to_broadcast([P, n, P])

        def cube(ap):
            return ap.rearrange("p (n s) -> p n s", s=P)

        k_t, q_t, v_t = room(0), room(1), room(2)
        z_t = room(3)
        conv_in = {"k": room(5), "q": room(6), "v": room(7)}
        conv_out = {"k": k_t, "q": q_t, "v": v_t}
        sc_c, sc_conv = room(8), room(11)
        sc_u, sc_tmp, y_sc = sc_c, (gate, silu), sc_conv
        diag = [room(5), room(6), room(4)]
        g_exp = room(12)
        decay = room(10)
        kb_t, qs_t, qg_t = room(3), room(11), room(4)
        lower, attn = room(9), room(5)
        kb_g, k_g, v_b = room(14), room(13), room(10)
        step_m = [room(6), room(1)]
        inv, inv_t = room(0), room(15)
        prod = sq[:, 0:2, :].rearrange("p a b -> p (a b)")
        u_sol, w_sol = room(6), room(2)
        state = [room(0)[:, 0:512], room(0)[:, 512:1024]]
        v_new = [room(1)[:, 0:512], room(1)[:, 512:1024]]
        o_gated, o_diag = room(8), room(9)

        tiny = sb("tiny", [P, 24, NS])
        (T_B, T_A, T_NEG, T_U, T_W, T_D, T_R, T_LN, T_G, T_EB, T_BETA, T_GC, T_GL, T_EGC, T_EKG, T_RK, T_RQ,
         T_R1, T_F1, T_F2, T_OS, T_Y, T_X, T_RO) = range(24)

        def ty(k):
            return tiny[:, k, :]

        wba_pad = room(13)
        wba_hi = m_hi[:, 0:4, :].rearrange("p a b -> p (a b)")
        wba_lo = m_lo[:, 0:4, :].rearrange("p a b -> p (a b)")
        ba_row = act[:, 0:SEQ]
        gate_par = sb("gate_par", [P, 3, HEADS])

        named = {}

        def mark(ins, name):
            if name not in named:
                named[name] = sem(name)
            ins.then_inc(named[name], 1)

        def need(eng, name, count=1):
            if name not in named:
                named[name] = sem(name)
            eng.wait_ge(named[name], count)

        def hyb_sync(sp):
            w = t["hyb_w_in"][0].rearrange("(k p) f -> p k f", p=P)
            for m in range(HYB_IN):
                load(sp, (first["hyb_in"] + m, 0), w[:, :, HYB_COLS[m]:HYB_COLS[m] + CW])
            w = t["hyb_w_out"][0].rearrange("(k p) f -> p k f", p=P)
            for m in range(HYB_OUT):
                load(sp, (first["hyb_out"] + m, 0), w[:, :, m * CW:(m + 1) * CW])

        HYB_PLAN = {(0, 1): ["gates"], (1, 1): ["gates_turned"], (2, 1): ["gates_logged"], (4, 1): ["scalars"], (5, 1): ["rows"],
                    (6, 1): ["products"], (7, 0): ["start"]}
        spots = [(7, 1)] + [(m, half) for m in range(8, HYB_IN) for half in range(2)]
        phases = [f"{x}{n}" for n in range(1, N_LEVEL) for x in ("left", "right")] + ["solutions", "add0", "read1"]
        for spot, name in zip(spots, phases):
            HYB_PLAN[spot] = [name]
        assert len(phases) == len(spots)
        LAST_STEP = TB * JC - 1

        def hyb_tensor_phase(pe, name):
            mm = nc.tensor.matmul
            if name == "gates":
                need(pe, "wba_split")
                for kt in range(KT):
                    cols = slice(kt * P, (kt + 1) * P)
                    mm(AUX2[:, 0:SEQ], wba_hi[:, cols], h_hi[:, kt, :], start=(kt == 0), stop=False)
                    mm(AUX2[:, 0:SEQ], wba_hi[:, cols], h_lo[:, kt, :], start=False, stop=False)
                    i = mm(AUX2[:, 0:SEQ], wba_lo[:, cols], h_hi[:, kt, :], start=False, stop=(kt == KT - 1))
                mark(i, "gates_projected")
            if name == "gates_turned":
                need(pe, "gates_scaled")
                for b in range(TB):
                    i = nc.tensor.transpose(AUX2[:, b * P:(b + 1) * P], ba_row[:, b * P:(b + 1) * P], ident)
                mark(i, "gates_turned")
            if name == "scalars":
                need(pe, "g_ready")
                mm(AUX2[:, 16:24], kon[:, K_TRI:K_TRI + P], ty(T_G), start=True, stop=True)
                i = mm(AUX2[:, 24:32], kon[:, K_BLK:K_BLK + P], ty(T_G), start=True, stop=True)
                mark(i, "g_summed")
                need(pe, "kq_silu", 4)
                for which, src in enumerate((k_t, q_t)):
                    for b in range(TB):
                        for h in range(HEADS):
                            i = nc.tensor.transpose(ACC[2 * which + b][:, h * P:(h + 1) * P],
                                                    by_tile(src)[:, h, b * P:(b + 1) * P], ident)
                mark(i, "kq_turned")
                need(pe, "diagonals", 1)
                need(pe, "g_copied")
                for n, bk in enumerate((AUX, AUX2)):
                    i = mm(bk[:], ones[:], diag[0][:, n * 512:(n + 1) * 512], start=True, stop=True)
                mark(i, "rows_summed")
            if name == "rows":
                for k, (b0, b1) in ((1, (ACC[2], ACC[3])), (2, (AUX, AUX2))):
                    need(pe, "diagonals", k + 1)
                    if k == 2:
                        need(pe, "decay_arg")
                        need(pe, "rows_exp", 3)
                    for n, bk in enumerate((b0, b1)):
                        i = mm(bk[:], ones[:], diag[k][:, n * 512:(n + 1) * 512], start=True, stop=True)
                    mark(i, "rows_summed")
            if name == "products":
                for k, (rhs, banks) in enumerate(((kb_t, ACC[2:4]), (qs_t, (AUX, AUX2)))):
                    need(pe, "kq_scaled", k + 1)
                    for b in range(TB):
                        for h in range(HEADS):
                            i = mm(banks[b][:, h * P:(h + 1) * P], by_tile(k_t)[:, h, b * P:(b + 1) * P],
                                   one(rhs, b, h), start=True, stop=True)
                    mark(i, "pairs_ready")
            if name == "start":
                need(pe, "pairs_masked", 2)
                need(pe, "inverse_t", 1)
                for b in range(TB):
                    for h in range(HEADS):
                        i = nc.tensor.transpose((AUX, AUX2)[b][:, h * P:(h + 1) * P], one(inv_t, b, h), ident)
                mark(i, "inverse_turned")
            if name[:4] == "left":
                n = int(name[4:])
                need(pe, "level_masked", n)
                need(pe, "inverse", n)
                for b in range(TB):
                    for h in range(HEADS):
                        i = mm((AUX, AUX2)[b][:, h * P:(h + 1) * P], one(step_m[n % 2], b, h), one(inv, b, h),
                               start=True, stop=True)
                    mark(i, "left_done")
            if name[:5] == "right":
                n = int(name[5:])
                if n == N_LEVEL - 1:
                    need(pe, "v_silu", 2)
                    for b in range(TB):
                        for h in range(HEADS):
                            i = nc.tensor.transpose(ACC[2 + b][:, h * P:(h + 1) * P],
                                                    by_tile(v_t)[:, h, b * P:(b + 1) * P], ident)
                    mark(i, "v_turned")
                for b in range(TB):
                    need(pe, "left_copied", TB * (n - 1) + b + 1)
                    if b == 0:
                        need(pe, "inverse_t", n)
                        need(pe, "k_scaled", 2)
                    for h in range(HEADS):
                        i = mm(ACC[b][:, h * P:(h + 1) * P], one(prod, b, h), one(inv_t, b, h), start=True,
                               stop=True)
                    if n < N_LEVEL - 1:
                        for h in range(HEADS):
                            i = mm(ACC[2 + b][:, h * P:(h + 1) * P], one(inv_t, b, h), one(prod, b, h),
                                   start=True, stop=True)
                    mark(i, "right_done")
            if name[:4] == "read":
                s = int(name[4:])
                b, j = divmod(s, JC)
                rows = slice(j * CHUNK, (j + 1) * CHUNK)
                need(pe, "solutions_copied", 2)
                need(pe, "state_ready", s)
                for h in range(HEADS):
                    i = mm(ACC[0][rows, h * P:(h + 1) * P], one(w_sol, b, h)[:, rows],
                           state[s % 2][:, h * P:(h + 1) * P], start=True, stop=True)
                mark(i, "state_read")
            if name[:3] == "add":
                s = int(name[3:])
                b, j = divmod(s, JC)
                rows = slice(j * CHUNK, (j + 1) * CHUNK)
                if s:
                    need(pe, "v_new_ready", s)
                else:
                    need(pe, "solutions_copied", 2)
                    need(pe, "qg_ready")
                vn = v_new[b] if s else u_sol
                if s < LAST_STEP:
                    for h in range(HEADS):
                        i = mm(ACC[1][:, h * P:(h + 1) * P], one(k_g, b, h)[rows, :], vn[rows, h * P:(h + 1) * P],
                               start=True, stop=True)
                    mark(i, "state_added")
                for h in range(HEADS):
                    dst = ACC[2 + b][:, h * P + j * CHUNK:h * P + (j + 1) * CHUNK]
                    if s:
                        mm(dst, state[s % 2][:, h * P:(h + 1) * P], one(qg_t, b, h)[:, rows], start=True,
                           stop=False)
                    i = mm(dst, vn[rows, h * P:(h + 1) * P], one(attn, b, h)[rows, rows], start=(s == 0), stop=True)
                if j == JC - 1:
                    mark(i, "o_ready")
            if name[:5] == "o_sum":
                b = int(name[5:])
                need(pe, "o_squared", b + 1)
                for h in range(HEADS):
                    i = mm(AUX2[:, h:h + 1], sq[:, 2 + b, h * P:(h + 1) * P], ones[:, 0:1], start=True, stop=True)
                mark(i, "o_summed")
            if name[:5] == "o_row":
                b = int(name[5:])
                need(pe, "o_diagonal", b + 1)
                mark(mm(AUX2[:], ones[:], o_diag[:, b * 512:(b + 1) * 512], start=True, stop=True), "o_rows")
            if name == "solutions":
                need(pe, "inverse_t", N_LEVEL)
                need(pe, "v_scaled")
                for k, (banks, what) in enumerate(((ACC[0:2], v_b), (ACC[2:4], kb_g))):
                    for b in range(TB):
                        for h in range(HEADS):
                            st, mv = one(inv_t, b, h), one(what, b, h)
                            if k:
                                st, mv = mv, st
                            i = mm(banks[b][:, h * P:(h + 1) * P], st, mv, start=True, stop=True)
                    mark(i, "solved")

        def hyb_vector_phase(dve, name):
            v = nc.vector

            def then(ins, k=[0]):
                mark(ins, "dve_step")
                named_steps[0] += 1
                need(dve, "dve_step", named_steps[0])

            if name == "gates":
                need(dve, "gates_projected")
                mark(v.tensor_tensor(ba_row[:], AUX2[:, 0:SEQ], rstd[:, 0:SEQ], ALU.mult), "gates_scaled")
            if name == "gates_turned":
                need(dve, "gates_turned")
                turned = AUX2[:, 0:2 * P].rearrange("p (b c) -> p b c", b=TB)
                v.tensor_copy(tiny[:, T_B, :].rearrange("p (b h) -> p b h", b=TB), turned[:, :, 0:HEADS])
                then(v.tensor_copy(tiny[:, T_A, :].rearrange("p (b h) -> p b h", b=TB),
                                   turned[:, :, HEADS:2 * HEADS]))
                for b in range(TB):
                    o = b * HEADS
                    i = v.tensor_tensor(tiny[:, T_Y, o:o + HEADS], tiny[:, T_A, o:o + HEADS], gate_par[:, 1, :],
                                        ALU.add)
                then(i)
                mark(v.scalar_tensor_tensor(out=ty(T_NEG), in0=ty(T_Y), scalar=-1.0, in1=ty(T_Y), op0=ALU.mult,
                                            op1=ALU.min), "minus_abs")
            if name == "gates_logged":
                need(dve, "log_w")
                then(v.tensor_scalar(ty(T_W), ty(T_U), 1.0, None, ALU.add))
                then(v.scalar_tensor_tensor(out=ty(T_D), in0=ty(T_W), scalar=-1.0, in1=ty(T_U), op0=ALU.add,
                                            op1=ALU.subtract))
                then(v.reciprocal(ty(T_R), ty(T_W)))
                then(v.tensor_tensor(ty(T_D), ty(T_D), ty(T_R), ALU.mult))
                then(v.tensor_tensor(ty(T_X), ty(T_LN), ty(T_D), ALU.subtract))
                then(v.scalar_tensor_tensor(out=ty(T_X), in0=ty(T_Y), scalar=0.0, in1=ty(T_X), op0=ALU.max,
                                            op1=ALU.add))
                for b in range(TB):
                    o = b * HEADS
                    i = v.scalar_tensor_tensor(out=tiny[:, T_G, o:o + HEADS], in0=tiny[:, T_X, o:o + HEADS],
                                               scalar=-1.0, in1=gate_par[:, 2, :], op0=ALU.mult, op1=ALU.mult)
                mark(i, "g_ready")
                need(dve, "g_ready")
                mark(v.tensor_tensor(cube(diag[0]), table(K_TRI, NS), wide(ty(T_G)), ALU.mult), "diagonals")
                then(v.tensor_scalar(ty(T_EB), ty(T_EB), 1.0, None, ALU.add))
                then(v.reciprocal(ty(T_BETA), ty(T_EB)))
            if name == "scalars":
                need(dve, "g_summed")
                v.tensor_copy(ty(T_GC), AUX2[:, 16:24])
                mark(v.tensor_copy(ty(T_GL), AUX2[:, 24:32]), "g_copied")
                need(dve, "g_copied")
                need(dve, "rows_summed", 1)
                for b in range(TB):
                    i = v.tensor_tensor(by_pair(decay, b), bank_pair((AUX, AUX2)[b]), spread(ty(T_GC), b),
                                        ALU.subtract)
                then(i)
                mark(v.tensor_scalar(decay, decay, 0.0, None, ALU.min), "decay_arg")
                need(dve, "kq_squared")
                then(v.tensor_reduce(tiny[:, T_RK:T_RQ + 1, :].rearrange("p k n -> p (k n)"),
                                     sq[:].rearrange("p b (h s) -> p (b h) s", s=P), AX.X, ALU.add))
                v.tensor_scalar(ty(T_RK), ty(T_RK), 1e-6, None, ALU.add)
                then(v.tensor_scalar(ty(T_RQ), ty(T_RQ), 1e-6, float(DK), ALU.add, ALU.mult))
                v.reciprocal(tiny[:, T_RK:T_RQ + 1, :], tiny[:, T_RK:T_RQ + 1, :])
                mark(v.tensor_tensor(ty(T_GL), ty(T_GL), ty(T_GC), ALU.subtract), "norms_inverted")
                need(dve, "norms_rooted")
                then(v.tensor_tensor(ty(T_R1), ty(T_RK), ty(T_BETA), ALU.mult))
                mark(v.tensor_tensor(cube(diag[1]), table(K_IDENT, NS), wide(ty(T_R1)), ALU.mult), "diagonals")
                mark(v.tensor_tensor(cube(diag[2]), table(K_IDENT, NS), wide(ty(T_RQ)), ALU.mult), "diagonals")
            if name == "rows":
                need(dve, "rows_exp", 1)
                then(v.tensor_tensor(cube(decay), cube(decay), wide(ty(T_RK)), ALU.mult))
                mark(v.tensor_tensor(cube(decay), cube(decay), table(K_TRI, NS), ALU.mult), "decay_ready")
                need(dve, "rows_summed", 2)
                for b in range(TB):
                    i = v.tensor_tensor(by_pair(kb_t, b), bank_pair(ACC[2 + b]),
                                        by_tile(k_t)[:, :, b * P:(b + 1) * P], ALU.mult)
                mark(i, "kq_scaled")
                need(dve, "rows_summed", 3)
                for b in range(TB):
                    i = v.tensor_tensor(by_pair(qs_t, b), bank_pair((AUX, AUX2)[b]),
                                        by_tile(q_t)[:, :, b * P:(b + 1) * P], ALU.mult)
                mark(i, "kq_scaled")
                need(dve, "gates_raised")
                v.tensor_tensor(ty(T_F2), ty(T_RK), ty(T_EKG), ALU.mult)
                then(v.scalar_tensor_tensor(out=ty(T_F1), in0=ty(T_R1), scalar=-1.0, in1=ty(T_EGC), op0=ALU.mult,
                                            op1=ALU.mult))
                for b in range(TB):
                    i = v.tensor_tensor(by_pair(k_g, b), bank_pair(ACC[b]), spread(ty(T_F2), b), ALU.mult)
                mark(i, "k_scaled")
                for b in range(TB):
                    i = v.tensor_tensor(by_pair(kb_g, b), bank_pair(ACC[b]), spread(ty(T_F1), b), ALU.mult)
                mark(i, "k_scaled")
            if name == "products":
                need(dve, "decay_ready")
                need(dve, "pairs_ready", 1)
                for b in range(TB):
                    i = v.tensor_tensor(by_pair(lower, b), bank_pair(ACC[2 + b]), by_pair(decay, b), ALU.mult)
                mark(i, "pairs_masked")
                need(dve, "pairs_masked", 1)
                then(v.tensor_tensor(cube(inv_t), cube(lower), table(K_LEVEL, NS), ALU.mult))
                mark(v.tensor_tensor(cube(inv_t), table(K_IDENT, NS), cube(inv_t), ALU.subtract), "inverse_t")
                need(dve, "pairs_ready", 2)
                for b in range(TB):
                    i = v.tensor_tensor(by_pair(attn, b), bank_pair((AUX, AUX2)[b]), by_pair(decay, b), ALU.mult)
                mark(i, "pairs_masked")
            if name == f"right{N_LEVEL - 1}":
                need(dve, "v_turned")
                for b in range(TB):
                    i = v.tensor_tensor(by_pair(v_b, b), bank_pair(ACC[2 + b]), spread(ty(T_BETA), b), ALU.mult)
                mark(i, "v_scaled")
            if name[:5] == "right":
                n = int(name[5:])
                for b in range(TB):
                    need(dve, "right_done", TB * (n - 1) + b + 1)
                    if n < N_LEVEL - 1:
                        i = v.tensor_tensor(by_pair(inv, b), by_pair(inv, b), bank_pair(ACC[2 + b]), ALU.subtract)
                if n < N_LEVEL - 1:
                    mark(i, "inverse")
                for b in range(TB):
                    i = v.tensor_tensor(by_pair(inv_t, b), by_pair(inv_t, b), bank_pair(ACC[b]), ALU.subtract)
                mark(i, "inverse_t")

            if name[:4] == "read":
                s = int(name[4:])
                b, j = divmod(s, JC)
                rows = slice(j * CHUNK, (j + 1) * CHUNK)
                need(dve, "state_read", s)
                mark(v.tensor_tensor(v_new[b][rows, :], ACC[0][rows, :], u_sol[rows, b * 512:(b + 1) * 512],
                                     ALU.add), "v_new_ready")
            if name[:3] == "add":
                s = int(name[3:])
                b, j = divmod(s, JC)
                last = j * CHUNK + CHUNK - 1
                new, old = state[(s + 1) % 2], state[s % 2]
                need(dve, "rows_exp", 3)
                need(dve, "state_added", s + 1)
                if s == 0:
                    i = v.tensor_copy(new, ACC[1][:])
                else:
                    for h in range(HEADS):
                        cols = slice(h * P, (h + 1) * P)
                        i = v.scalar_tensor_tensor(out=new[:, cols], in0=old[:, cols],
                                                   scalar=one(g_exp, b, h)[:, last:last + 1],
                                                   in1=ACC[1][:, cols], op0=ALU.mult, op1=ALU.add)
                mark(i, "state_ready")
                need(dve, "state_ready", s + 1)

        named_steps = [0]

        def hyb_scalar_phase(act_e, name):
            a = nc.scalar.activation

            if name == "gates_turned":
                mark(a(gate_par[:, 2, :], gate_par[:, 0, :], ACT.Exp), "gates_exp_par")
                need(act_e, "minus_abs")
                a(ty(T_EB), ty(T_B), ACT.Exp, scale=-1.0)
                mark(a(ty(T_U), ty(T_NEG), ACT.Exp), "gates_exp")
                need(act_e, "gates_exp")
                mark(a(ty(T_LN), ty(T_U), ACT.Ln, bias=1.0), "log_w")
            if name == "scalars":
                need(act_e, "kq_turned")
                for k in range(2 * TB):
                    i = a(sq[:, k, :], ACC[k][:], ACT.Square)
                mark(i, "kq_squared")
                need(act_e, "norms_inverted")
                mark(a(tiny[:, T_RK:T_RQ + 1, :], tiny[:, T_RK:T_RQ + 1, :], ACT.Sqrt), "norms_rooted")
                a(ty(T_EGC), ty(T_GC), ACT.Exp)
                mark(a(ty(T_EKG), ty(T_GL), ACT.Exp), "gates_raised")
                need(act_e, "decay_arg")
                mark(a(decay, decay, ACT.Exp), "rows_exp")
                for b in range(TB):
                    mark(a(by_pair(g_exp, b), bank_pair((AUX, AUX2)[b]), ACT.Exp), "rows_exp")
            if name == "start":
                need(act_e, "inverse_turned")
                for b in range(TB):
                    i = a(by_pair(inv, b), bank_pair((AUX, AUX2)[b]), ACT.Copy)
                mark(i, "inverse")
            if name[:4] == "left":
                n = int(name[4:])
                for b in range(TB):
                    need(act_e, "left_done", TB * (n - 1) + b + 1)
                    mark(a(by_pair(prod, b), bank_pair((AUX, AUX2)[b]), ACT.Copy), "left_copied")
            if name == "solutions":
                for k, (banks, dst) in enumerate(((ACC[0:2], u_sol), (ACC[2:4], w_sol))):
                    need(act_e, "solved", k + 1)
                    for b in range(TB):
                        i = a(by_pair(dst, b), bank_pair(banks[b]), ACT.Copy)
                    mark(i, "solutions_copied")

        def hyb_pool_phase(pool, name):
            if name == "rows":
                need(pool, "kq_scaled", 2)
                need(pool, "rows_exp", 3)
                mark(nc.gpsimd.tensor_tensor(qg_t, qs_t, g_exp, ALU.mult), "qg_ready")
            if name == "products":
                need(pool, "pairs_masked", 2)
                need(pool, "qg_ready")
            if name == "start" or name[:4] == "left":
                n = 1 if name == "start" else int(name[4:]) + 1
                if n < N_LEVEL:
                    if n > 2:
                        need(pool, "left_done", TB * (n - 2))
                    if n == 1:
                        need(pool, "kq_scaled", 2)
                    mark(nc.gpsimd.tensor_tensor(cube(step_m[n % 2]), cube(lower), table(K_LEVEL + P * n, NS),
                                                 ALU.mult), "level_masked")

        def hyb_tensor(pe, n):
            c = first["hyb_in"]
            pe.wait_ge(rest_loaded, 16 * 5)
            for m in range(HYB_IN):
                if m >= 2:
                    pe.wait_ge(hyb_evacuated, m - 1)
                halfway = HYB_PLAN.get((m, 0), [])
                column_chunk(pe, (c + m, 0), (GATE, UP)[m % 2], h_hi, h_lo,
                             (h_ready, PAIRS * n) if m == 0 else None,
                             (lambda: [hyb_tensor_phase(pe, x) for x in halfway]) if halfway else None)
                if m == 0:
                    norm_ss(pe, n)
                for x in HYB_PLAN.get((m, 1), []):
                    hyb_tensor_phase(pe, x)

            mm = nc.tensor.matmul

            def out_part(j, tiles, fts, opens, toks=slice(0, SEQ)):
                ch = (first["hyb_out"] + j, 0)
                pe.wait_ge(lo_split, number(ch) + 1)
                for ft in fts:
                    for kt in tiles:
                        i = product(OUT_BANKS[j][:, ft * SEQ + toks.start:ft * SEQ + toks.stop], slot(ch),
                                    slice(kt * CW + ft * P, kt * CW + (ft + 1) * P), m_hi[:, kt, toks],
                                    m_lo[:, kt, toks], start=(opens and ft == 0 and kt == tiles[0]))
                return i

            pe.wait_ge(hyb_evacuated, HYB_IN)
            need(pe, "conv_split")
            conv_tiles, head_tiles = [4, 5, 6, 7], [0, 1, 2, 3]
            out_part(0, conv_tiles, [0], True)
            hyb_tensor_phase(pe, "add1")
            out_part(0, conv_tiles, [1], False)
            hyb_tensor_phase(pe, "read2")
            hyb_tensor_phase(pe, "o_sum0")
            out_part(1, conv_tiles, [0], True)
            hyb_tensor_phase(pe, "add2")
            hyb_tensor_phase(pe, "o_row0")
            out_part(1, conv_tiles, [1], False)
            hyb_tensor_phase(pe, "read3")
            out_part(2, conv_tiles, [0], True)
            hyb_tensor_phase(pe, "add3")
            out_part(2, conv_tiles, [1], False)
            hyb_tensor_phase(pe, "o_sum1")
            toks = [slice(b * P, (b + 1) * P) for b in range(TB)]
            need(pe, "o_split", 1)
            out_part(0, head_tiles, range(HG), False, toks[0])
            hyb_tensor_phase(pe, "o_row1")
            out_part(1, head_tiles, range(HG), False, toks[0])
            out_part(2, head_tiles, range(HG), False, toks[0])
            need(pe, "o_split", TB)
            for j in range(RING):
                out_part(j, head_tiles, range(HG), False, toks[1]).then_inc(w_used, 1)
            out_part(RING, conv_tiles + head_tiles, range(HG), True).then_inc(w_used, 1)

        def hyb_scalar(act_e, n):
            c = first["hyb_in"]
            for m in range(HYB_IN):
                for x in HYB_PLAN.get((m, 0), []):
                    hyb_scalar_phase(act_e, x)
                if m < HYB_IN:
                    split_hi(act_e, (c + m + RING, 0))
                kind = KINDS[m // 2]
                if m >= 4:
                    for x in HYB_PLAN.get((m, 1), []):
                        hyb_scalar_phase(act_e, x)
                if kind in conv_out:
                    need(act_e, kind + "_conv_done", m % 2 + 1)
                    tile = conv_out[kind][:, (m % 2) * 512:(m % 2 + 1) * 512]
                    mark(nc.scalar.activation(tile, tile, ACT.Silu), "v_silu" if kind == "v" else "kq_silu")
                if m >= 12:
                    act_e.wait_ge(hyb_evacuated, m + 1)
                    o = (m - 12) * 512
                    mark(nc.scalar.activation(z_t[:, o:o + 512], z_t[:, o:o + 512], ACT.Silu), "z_silu")
                if m == 12:
                    need(act_e, "conv_gated", 2)
                    mark(nc.scalar.activation(m_hi[:, 4:8, :].rearrange("p a b -> p (a b)"), y_sc, ACT.Copy),
                         "conv_hi")
                if m < 4:
                    for x in HYB_PLAN.get((m, 1), []):
                        hyb_scalar_phase(act_e, x)
            for b in range(TB):
                need(act_e, "o_ready", b + 1)
                mark(nc.scalar.activation(sq[:, 2 + b, :], ACC[2 + b][:], ACT.Square), "o_squared")
                need(act_e, "o_inverted", b + 1)
                o = b * HEADS
                mark(nc.scalar.activation(tiny[:, T_RO, o:o + HEADS], tiny[:, T_OS, o:o + HEADS], ACT.Sqrt),
                     "o_rooted")
                need(act_e, "o_final", b + 1)
                mark(nc.scalar.activation(m_hi[:, 0:4, b * P:(b + 1) * P], by_tile(o_gated)[:, :, b * P:(b + 1) * P],
                                          ACT.Copy), "o_hi")

        def hyb_vector(dve, n):
            v = nc.vector
            c = first["hyb_in"]

            def then(ins):
                mark(ins, "dve_step")
                named_steps[0] += 1
                need(dve, "dve_step", named_steps[0])

            dve.wait_ge(rest_loaded, 16 * 5)

            def evacuate(m, dst):
                dve.wait_ge(w_used, c + m + 1)
                i = v.tensor_tensor(dst.rearrange("p (a s) -> p a s", a=2),
                                    (GATE, UP)[m % 2][:].rearrange("p (a s) -> p a s", a=2),
                                    over_rows(rstd[:, 0:SEQ], 2), ALU.mult)
                i.then_inc(hyb_evacuated, 1)

            def conv(src, dst, taps, weight, tiles, done):
                for s in range(taps):
                    for x in tiles:
                        a, d = src[:, x * SEQ:(x + 1) * SEQ], dst[:, x * SEQ:(x + 1) * SEQ]
                        if s == 0:
                            i = v.tensor_scalar(d, a, weight(s, x), None, ALU.mult)
                        else:
                            i = v.scalar_tensor_tensor(out=d[:, s:], in0=a[:, 0:SEQ - s], scalar=weight(s, x),
                                                       in1=d[:, s:], op0=ALU.mult, op1=ALU.add)
                    if s < taps - 1:
                        then(i)
                    else:
                        mark(i, done)

            for m in range(HYB_IN):
                for x in HYB_PLAN.get((m, 0), []):
                    hyb_vector_phase(dve, x)
                o = (m % 2) * 512
                span = slice(o, o + 512)
                tiles = (2 * (m % 2), 2 * (m % 2) + 1)
                kind = KINDS[m // 2]
                evacuate(m, {"c": sc_c, "z": z_t}[kind][:, span] if kind in "cz" else
                         conv_in[kind][:, span] if kind in conv_in else sc_tmp[m % 2][:])
                if m >= 4:
                    for x in HYB_PLAN.get((m, 1), []):
                        hyb_vector_phase(dve, x)
                if kind in conv_in:
                    dve.wait_ge(hyb_evacuated, m + 1)
                    base = V_CONV + {"k": 4, "q": 0, "v": 8}[kind]
                    conv(conv_in[kind], conv_out[kind], 4,
                         lambda s, x: vecT[:, base + 12 * (3 - s) + x:base + 12 * (3 - s) + x + 1],
                         tiles, kind + "_conv_done")
                if kind == "h":
                    dve.wait_ge(hyb_evacuated, m + 1)
                    then(v.tensor_tensor(sc_u[:, span], sc_tmp[m % 2][:], sc_c[:, span], ALU.mult))
                    conv(sc_u, sc_conv, 3, lambda s, x: vecT[:, V_SC + 4 * (2 - s) + x:V_SC + 4 * (2 - s) + x + 1],
                         tiles, "sc_conv_done")
                if kind == "b":
                    dve.wait_ge(hyb_evacuated, m + 1)
                    need(dve, "sc_conv_done", m % 2 + 1)
                    mark(v.tensor_tensor(y_sc[:, span], sc_tmp[m % 2][:], sc_conv[:, span], ALU.mult), "conv_gated")
                if m == 12:
                    need(dve, "conv_hi")
                    mark(v.tensor_tensor(m_lo[:, 4:8, :].rearrange("p a b -> p (a b)"), y_sc,
                                         m_hi[:, 4:8, :].rearrange("p a b -> p (a b)").bitcast(F32),
                                         ALU.subtract), "conv_split")
                if m < 4:
                    for x in HYB_PLAN.get((m, 1), []):
                        hyb_vector_phase(dve, x)

            def o_scale(b):
                o = b * HEADS
                need(dve, "o_summed", b + 1)
                then(v.tensor_scalar(tiny[:, T_OS, o:o + HEADS], AUX2[:, 0:HEADS], 1.0 / DK, EPS, ALU.mult, ALU.add))
                mark(v.reciprocal(tiny[:, T_OS, o:o + HEADS], tiny[:, T_OS, o:o + HEADS]), "o_inverted")

            def o_spread(b):
                need(dve, "o_rooted", b + 1)
                mark(v.tensor_tensor(by_pair(o_diag, b), table(K_IDENT, HEADS), spread(ty(T_RO), b), ALU.mult),
                     "o_diagonal")

            def o_gate(b):
                need(dve, "z_weighted")
                need(dve, "o_squared", b + 1)
                mark(v.tensor_tensor(by_tile(o_gated)[:, :, b * P:(b + 1) * P], bank_pair(ACC[2 + b]),
                                     by_tile(z_t)[:, :, b * P:(b + 1) * P], ALU.mult), "o_gated")

            def o_finish(b):
                need(dve, "o_rows", b + 1)
                need(dve, "o_gated", b + 1)
                part = by_tile(o_gated)[:, :, b * P:(b + 1) * P]
                mark(v.tensor_tensor(part, part, bank_pair(AUX2), ALU.mult), "o_final")

            def o_rest(b):
                need(dve, "o_final", b + 1)
                need(dve, "o_hi", b + 1)
                mark(v.tensor_tensor(m_lo[:, 0:4, b * P:(b + 1) * P], by_tile(o_gated)[:, :, b * P:(b + 1) * P],
                                     m_hi[:, 0:4, b * P:(b + 1) * P].bitcast(F32), ALU.subtract), "o_split")

            hyb_vector_phase(dve, "add1")
            hyb_vector_phase(dve, "read2")
            o_scale(0)
            o_spread(0)
            o_gate(0)
            hyb_vector_phase(dve, "add2")
            o_finish(0)
            hyb_vector_phase(dve, "read3")
            o_rest(0)
            o_gate(1)
            o_scale(1)
            o_spread(1)
            o_finish(1)
            o_rest(1)

        def hyb_pool(pool):
            for m in range(HYB_IN):
                for x in HYB_PLAN.get((m, 0), []):
                    hyb_pool_phase(pool, x)
                split_lo(pool, (first["hyb_in"] + m + RING, 0), nc.gpsimd, handed_over=(m == 0))
                for x in HYB_PLAN.get((m, 1), []):
                    hyb_pool_phase(pool, x)
            need(pool, "z_silu", 2)
            mark(nc.gpsimd.tensor_scalar(z_t, z_t, vecT[:, V_GN:V_GN + 1], None, ALU.mult), "z_weighted")

        hyb_evacuated = sem("hyb_evacuated")

        HD = 64
        KV = t["swa_w_qkv"].shape[2] // HD // 6
        GRP = 4
        QW = KV * GRP * HD
        SWA_COLS = [QW, QW + CW] + [g * CW for g in range(KV)]
        SCALE = float(HD) ** -0.5
        b_qkv = work[:, 0:QW + 2 * CW]
        k_pad = work[:, 1536:3072].rearrange("p (b g d) -> p b g d", b=TB, g=KV)
        v_tok = work[:, 3072:3584].rearrange("p (b c) -> p b c", b=TB)
        q_tok = [work[:, 3584 + 512 * n:4096 + 512 * n] for n in range(2)]
        qT = [work[:, 4608 + 512 * n:5120 + 512 * n] for n in range(2)]
        kT = [work[:, 5632 + 1024 * n:6656 + 1024 * n] for n in range(2)]
        score = [work[:, 7680 + 1536 * n:9216 + 1536 * n] for n in range(2)]
        prob_t = [work[:, 10752:12288], work[:, 13504:15040]]
        o_tok = [work[:, 12288 + 512 * n:12800 + 512 * n] for n in range(2)]
        sinks = sb("swa_sink_cols", [P, KV * GRP])
        att = work[:, 13312:13312 + 48 * KV].rearrange("p (k n h) -> p k n h", k=6, h=GRP)
        A_MAX, A_NEG, A_SUM, A_SINK, A_DEN, A_INV = range(6)

        def stat(k, g, b=None):
            if b is None:
                return att[:, k, 2 * g:2 * g + 2, :]
            return att[:, k, 2 * g + b, :]

        def score_part(g, b):
            s = score[g % 2]
            return (s[:, 0:512] if b == 0 else s[:, 512:1536]).rearrange("p (h k) -> p h k", h=GRP)

        def head_tok(ap):
            return ap.rearrange("p (b h d) -> p b h d", b=TB, d=HD)

        def angles(col, lo, hi):
            a = kon[:, col:col + 128].rearrange("p (b h d) -> p b h d", b=TB, h=1)[:, :, :, lo:hi]
            return a.to_broadcast([P, TB, GRP, hi - lo])

        def swa_sync(sp):
            w = t["swa_w_qkv"][0].rearrange("(k p) f -> p k f", p=P)
            for m in range(SWA_IN):
                if m == 1:
                    sp.wait_ge(w_used, first["ffn2"] + 1)
                    sp.dma_start(b_qkv, t["swa_b_qkv"][0].partition_broadcast(P)).then_inc(bias_loaded, 16)
                load(sp, (first["swa_in"] + m, 0), w[:, :, SWA_COLS[m]:SWA_COLS[m] + CW])
            w = t["swa_w_o"][0].rearrange("(k p) f -> p k f", p=P)
            for m in range(SWA_OUT):
                load(sp, (first["swa_out"] + m, 0), w[:, :, m * CW:(m + 1) * CW])

        def swa_tensor(pe, n):
            c = first["swa_in"]
            mm, turn = nc.tensor.matmul, nc.tensor.transpose

            def token_chunk(m, half=None):
                if m >= 2:
                    pe.wait_ge(swa_evacuated, m - 1)
                ch = (c + m, 0)
                pe.wait_ge(lo_split, number(ch) + 1)
                bk, s = (GATE, UP)[m % 2], slot(ch)
                order = [(kt, b) for kt in range(KT) for b in range(TB)] if m == 0 else \
                    [(kt, b) for b in range(TB) for kt in range(KT)]
                for k, (kt, b) in enumerate(order):
                    if m == 0 and b == 0 and kt % 2 == 0:
                        pe.wait_ge(h_ready, PAIRS * n + kt // 2 + 1)
                    if half is not None and k == KT:
                        half()
                    for r, (st, mv) in enumerate(((h_hi, w_hi), (h_lo, w_hi), (h_hi, w_lo))):
                        i = mm(bk[:, b * CW:(b + 1) * CW], st[:, kt, b * P:(b + 1) * P],
                               mv[s][:, kt * CW:(kt + 1) * CW], start=(k + r == 0), stop=(kt == KT - 1 and r == 2),
                               skip_group_check=True)
                i.then_inc(w_used, 1)

            def turn_k():
                need(pe, "k_rotated")
                need(pe, "k_padded")
                for par in range(2):
                    for b in range(TB):
                        if par:
                            need(pe, "k_copied", b + 1)
                        for g in range(KV):
                            o = 64 * (1 - par)
                            i = turn((AUX, AUX2)[b][:, g * P:(g + 1) * P], k_pad[:, b, g, o:o + P], ident)
                        mark(i, "k_transposed")

            def turn_q(g):
                need(pe, "q_rotated", g + 1)
                if g:
                    need(pe, "q_copied", g)
                else:
                    need(pe, "k_copied", 3)
                for x in range(2):
                    for b in range(TB):
                        i = turn(AUX[:, x * SEQ + b * P:x * SEQ + (b + 1) * P],
                                 q_tok[g % 2][:, b * CW + x * P:b * CW + (x + 1) * P], ident)
                mark(i, "q_transposed")

            def scores(g):
                if g == 0:
                    need(pe, "k_copied", 4)
                elif g == 1:
                    need(pe, "scores_read", 1)
                else:
                    need(pe, "prob_copied", 2 * (g - 1))
                need(pe, "q_copied", g + 1)
                for h in range(GRP):
                    q = qT[g % 2][:, (h // 2) * SEQ:(h // 2 + 1) * SEQ]
                    k = kT[h % 2][:, g * SEQ:(g + 1) * SEQ]
                    mm(ACC[h // 2][:, (h % 2) * SEQ:(h % 2 + 1) * SEQ], q[:, P:2 * P], k, start=True, stop=True)
                for h in range(GRP):
                    q = qT[g % 2][:, (h // 2) * SEQ:(h // 2 + 1) * SEQ]
                    k = kT[h % 2][:, g * SEQ:(g + 1) * SEQ]
                    i = mm(ACC[2][:, h * P:(h + 1) * P], q[:, 0:P], k[:, 0:P], start=True, stop=True)
                mark(i, "scores_ready")

            def turn_probs(g):
                need(pe, "probs_ready", g + 1)
                if g < KV - 1:
                    need(pe, "scores_read", g + 2)
                else:
                    need(pe, "prob_copied", 2 * g)
                for kb in range(2):
                    for h in range(GRP):
                        i = turn(ACC[kb][:, h * P:(h + 1) * P], score_part(g, 1)[:, h, kb * P:(kb + 1) * P], ident)
                for h in range(GRP):
                    i = turn(ACC[2][:, h * P:(h + 1) * P], score_part(g, 0)[:, h, :], ident)
                mark(i, "probs_transposed")

            def values(g):
                need(pe, "prob_copied", 2 * g + 2)
                if g:
                    need(pe, "o_normed", g)
                for h in range(GRP):
                    def p_t(k):
                        return prob_t[g % 2][:, k * 512 + h * P:k * 512 + (h + 1) * P]
                    v = v_tok[:, :, g * HD:(g + 1) * HD]
                    mm(ACC[3][:, CW + h * HD:CW + (h + 1) * HD], p_t(0), v[:, 0, :], start=True, stop=False)
                    mm(ACC[3][:, CW + h * HD:CW + (h + 1) * HD], p_t(1), v[:, 1, :], start=False, stop=True)
                    i = mm(ACC[3][:, h * HD:(h + 1) * HD], p_t(2), v[:, 0, :], start=True, stop=True)
                mark(i, "values_summed")

            def turn_o(g):
                need(pe, "o_normed", g + 1)
                if g:
                    need(pe, "o_lo_done", g)
                for x in range(2):
                    for b in range(TB):
                        i = turn(AUX2[:, x * SEQ + b * P:x * SEQ + (b + 1) * P],
                                 o_tok[g % 2][:, b * CW + x * P:b * CW + (x + 1) * P], ident)
                mark(i, "o_transposed")

            def out_part(j, g, tiles):
                ch = (first["swa_out"] + j, 0)
                pe.wait_ge(lo_split, number(ch) + 1)
                need(pe, "o_lo_done", g + 1)
                for ft in range(HG):
                    for kt in tiles:
                        i = product(OUT_BANKS[j][:, ft * SEQ:(ft + 1) * SEQ], slot(ch),
                                    slice(kt * CW + ft * P, kt * CW + (ft + 1) * P), m_hi[:, kt, :], m_lo[:, kt, :],
                                    start=(ft == 0 and kt == 0))
                return i

            def out(g, j):
                if j == 2 and g == 0:
                    need(pe, "q_copied", KV)
                i = out_part(j, g, [2 * g, 2 * g + 1])
                if g == KV - 1:
                    i.then_inc(w_used, 1)

            token_chunk(0)
            norm_ss(pe, n)
            token_chunk(1)
            token_chunk(2, turn_k)
            token_chunk(3, lambda: turn_q(0))
            scores(0)
            token_chunk(4, lambda: turn_q(1))
            scores(1)
            token_chunk(5, lambda: (turn_q(2), turn_probs(0)))
            scores(2)
            values(0)
            turn_q(3)
            turn_probs(1)
            turn_o(0)
            scores(3)
            pe.wait_ge(swa_evacuated, SWA_IN)
            out(0, 0)
            out(0, 1)
            values(1)
            turn_probs(2)
            out(0, 2)
            turn_o(1)
            values(2)
            out(1, 0)
            turn_probs(3)
            out(1, 1)
            turn_o(2)
            out(1, 2)
            values(3)
            out(2, 0)
            turn_o(3)
            out(2, 1)
            out(2, 2)
            for j in range(RING):
                out(3, j)
            i = out_part(RING, KV - 1, range(KT))
            i.then_inc(w_used, 1)

        def swa_scalar(act_e, n):
            a = nc.scalar.activation
            c = first["swa_in"]

            def copy_k():
                for par in range(2):
                    for b in range(TB):
                        need(act_e, "k_transposed", 2 * par + b + 1)
                        dst = kT[par].rearrange("p (g s) -> p g s", g=KV)[:, :, b * P:(b + 1) * P]
                        mark(a(dst, (AUX, AUX2)[b][:].rearrange("p (g s) -> p g s", g=KV), ACT.Copy), "k_copied")

            def copy_q(g):
                need(act_e, "q_transposed", g + 1)
                if g >= 2:
                    need(act_e, "scores_ready", g - 1)
                mark(a(qT[g % 2], AUX[:], ACT.Copy), "q_copied")

            def exps(g):
                need(act_e, "max_ready", g + 1)
                a(stat(A_DEN, g), stat(A_SINK, g), ACT.Exp)
                for b in range(TB):
                    for h in range(GRP):
                        s = score_part(g, b)[:, h, :]
                        i = a(s, s, ACT.Exp, bias=stat(A_NEG, g, b)[:, h:h + 1], scale=SCALE,
                              accum_out=stat(A_SUM, g, b)[:, h:h + 1])
                mark(i, "probs_ready")

            def copy_probs(g):
                need(act_e, "probs_transposed", g + 1)
                if g >= 2:
                    need(act_e, "values_summed", g - 1)
                for k in range(2):
                    i = a(prob_t[g % 2][:, k * 512:(k + 1) * 512], ACC[k][:], ACT.Copy)
                mark(i, "prob_copied")

            def hi_o(g):
                need(act_e, "o_transposed", g + 1)
                mark(a(m_hi[:, 2 * g:2 * g + 2, :].rearrange("p a b -> p (a b)"), AUX2[:], ACT.Copy), "o_hi_done")

            for m in range(SWA_IN):
                if m == 2:
                    copy_k()
                if m >= 3:
                    copy_q(m - 3)
                if m == 4:
                    exps(0)
                if m == 5:
                    copy_probs(0)
                    exps(1)
                split_hi(act_e, (c + m + RING, 0))
            copy_q(3)
            copy_probs(1)
            hi_o(0)
            exps(2)
            exps(3)
            copy_probs(2)
            hi_o(1)
            copy_probs(3)
            hi_o(2)
            hi_o(3)

        def swa_vector(dve, n):
            v = nc.vector
            c = first["swa_in"]

            def then(ins):
                mark(ins, "dve_step")
                named_steps[0] += 1
                need(dve, "dve_step", named_steps[0])

            def evacuate(m, dst):
                dve.wait_ge(w_used, c + m + 1)
                if m == 0:
                    dve.wait_ge(bias_loaded, 16)
                for b in range(TB):
                    i = v.scalar_tensor_tensor(out=dst[:, b * CW:(b + 1) * CW],
                                               in0=(GATE, UP)[m % 2][:, b * CW:(b + 1) * CW],
                                               scalar=rstd[:, SEQ + b:SEQ + b + 1],
                                               in1=b_qkv[:, SWA_COLS[m]:SWA_COLS[m] + CW], op0=ALU.mult, op1=ALU.add)
                i.then_inc(swa_evacuated, 1)

            def rotate(m, dst, done):
                dve.wait_ge(swa_evacuated, m + 1)
                x, s = head_tok(gate[:]), head_tok(silu_r[:])
                h = HD // 2
                v.tensor_tensor(s[:, :, :, 0:h], x[:, :, :, h:HD], angles(K_SIN, 0, h), ALU.mult)
                then(v.tensor_tensor(s[:, :, :, h:HD], x[:, :, :, 0:h], angles(K_SIN, h, HD), ALU.mult))
                need(dve, "x_cos", 1 if m == 0 else m)
                for b in range(TB):
                    i = v.tensor_tensor(dst(b), head_tok(silu[:])[:, b], s[:, b], ALU.add)
                mark(i, done)

            def soft(g):
                need(dve, "scores_ready", g + 1)
                if g >= 2:
                    need(dve, "probs_transposed", g - 1)
                for k in range(2):
                    v.tensor_tensor(score_part(g, 1)[:, 2 * k:2 * k + 2, :],
                                    ACC[k][:].rearrange("p (h k) -> p h k", h=2),
                                    kon[:, K_ATT1:K_ATT1 + 256].rearrange("p (a k) -> p a k", a=1)
                                    .to_broadcast([P, 2, 256]), ALU.add)
                mark(v.tensor_tensor(score_part(g, 0), ACC[2][:].rearrange("p (h k) -> p h k", h=GRP),
                                     table(K_ATT0, GRP), ALU.add), "scores_read")
                need(dve, "scores_read", g + 1)
                for b in range(TB):
                    i = v.tensor_reduce(stat(A_MAX, g, b), score_part(g, b), AX.X, ALU.max)
                then(i)
                for b in range(TB):
                    i = v.scalar_tensor_tensor(out=stat(A_MAX, g, b), in0=stat(A_MAX, g, b), scalar=SCALE,
                                               in1=sinks[:, g * GRP:(g + 1) * GRP], op0=ALU.mult, op1=ALU.max)
                then(i)
                for b in range(TB):
                    v.tensor_tensor(stat(A_SINK, g, b), sinks[:, g * GRP:(g + 1) * GRP], stat(A_MAX, g, b),
                                    ALU.subtract)
                mark(v.tensor_scalar(stat(A_NEG, g), stat(A_MAX, g), -1.0, None, ALU.mult), "max_ready")

            def copy_probs(g):
                need(dve, "prob_copied", 2 * g + 1)
                mark(v.tensor_copy(prob_t[g % 2][:, 1024:1536], ACC[2][:]), "prob_copied")
                then(v.tensor_tensor(stat(A_DEN, g), stat(A_DEN, g), stat(A_SUM, g), ALU.add))
                mark(v.reciprocal(stat(A_INV, g), stat(A_DEN, g)), "den_ready")

            def norm_o(g):
                need(dve, "values_summed", g + 1)
                need(dve, "den_ready", g + 1)
                if g >= 2:
                    need(dve, "o_transposed", g - 1)
                for b in range(TB):
                    inv_b = stat(A_INV, g, b).rearrange("p (h d) -> p h d", d=1).to_broadcast([P, GRP, HD])
                    i = v.tensor_tensor(head_tok(o_tok[g % 2])[:, b],
                                        ACC[3][:].rearrange("p (b h d) -> p b h d", b=TB, h=GRP)[:, b], inv_b,
                                        ALU.mult)
                mark(i, "o_normed")

            def lo_o(g):
                need(dve, "o_hi_done", g + 1)
                mark(v.tensor_tensor(m_lo[:, 2 * g:2 * g + 2, :].rearrange("p a b -> p (a b)"), AUX2[:],
                                     m_hi[:, 2 * g:2 * g + 2, :].rearrange("p a b -> p (a b)").bitcast(F32),
                                     ALU.subtract), "o_lo_done")

            need(dve, "k_padded")
            for m in range(SWA_IN):
                if m == 1:
                    evacuate(m, work[:, 3072:3584])
                else:
                    if m > 2:
                        need(dve, "x_cos", m - 1)
                    evacuate(m, gate[:])
                if m == 0:
                    rotate(m, lambda b: k_pad[:, b, :, HD:2 * HD], "k_rotated")
                if m >= 2:
                    g = m - 2
                    if g >= 2:
                        need(dve, "q_transposed", g - 1)
                    rotate(m, lambda b: head_tok(q_tok[g % 2])[:, b], "q_rotated")
                if m == 3:
                    soft(0)
                if m == 4:
                    soft(1)
                    copy_probs(0)
            soft(2)
            norm_o(0)
            copy_probs(1)
            lo_o(0)
            soft(3)
            norm_o(1)
            copy_probs(2)
            lo_o(1)
            norm_o(2)
            copy_probs(3)
            lo_o(2)
            norm_o(3)
            lo_o(3)

        def swa_pool(pool):
            for m in range(SWA_IN):
                if m != 1:
                    pool.wait_ge(swa_evacuated, m + 1)
                    if m:
                        need(pool, "k_rotated") if m == 2 else need(pool, "q_rotated", m - 2)
                    mark(nc.gpsimd.tensor_tensor(head_tok(silu[:]), head_tok(gate[:]), angles(K_COS, 0, HD),
                                                 ALU.mult), "x_cos")
                split_lo(pool, (first["swa_in"] + m + RING, 0), nc.gpsimd, handed_over=(m == 0))

        swa_evacuated = sem("swa_evacuated")
        bias_loaded = sem("bias_loaded")

        def load_rest(act_e):
            act_e.dma_start(kon[:, P:K_END], t["constants"][:, P:K_END]).then_inc(rest_loaded, 16)
            act_e.dma_start(sinks[:], t["swa_sinks"][0].partition_broadcast(P)).then_inc(rest_loaded, 16)
            act_e.dma_start(gate_par[:, 0, :], t["gdn_a_log"][0].partition_broadcast(P)).then_inc(rest_loaded, 16)
            act_e.dma_start(gate_par[:, 1, :], t["gdn_dt_bias"][0].partition_broadcast(P)).then_inc(rest_loaded, 16)
            need(act_e, "wba_cleared")
            act_e.dma_start(wba_pad.rearrange("p (k c) -> p k c", k=KT)[:, :, 0:8],
                            t["hyb_w_in"][0].rearrange("(k p) f -> p k f", p=P)[:, :, 4 * KEY:4 * KEY + 8]) \
                 .then_inc(rest_loaded, 16)

        stages = [("ffn", 0), ("hyb", 0), ("ffn", 1), ("ffn", 2), ("swa", 0), ("ffn", 3)]
        stages = [x for x in stages if x[0] == "ffn" or mix[("hyb", "swa").index(x[0])]]

        def update(n):
            if n == 0:
                return ACC, [(acc_done, j + 1) for j in range(PAIRS)]
            kind, f = stages[n - 1]
            if kind == "ffn":
                base = PAIRS + (PAIRS - 1) * f
                end = first[f"ffn{f}"] + FFN_CHUNKS
                return ACC, [(acc_done, base + j + 1) for j in range(PAIRS - 1)] + [(w_used, end)]
            c = first[kind + "_out"]
            return OUT_BANKS, [(w_used, c + j + 1) for j in range(PAIRS)]

        block = ctx.enter_context(nc.Block())

        @block.sync
        def _(sp):
            xt = t["x"][0].rearrange("(b p) d -> p b d", p=P)
            sp.dma_start(kon[:, 0:P], t["constants"][:, 0:P]).then_inc(x_loaded, 16)
            sp.dma_start(x_in[:, :, 0:D // 2], xt[:, :, 0:D // 2]).then_inc(x_loaded, 16)
            sp.dma_start(x_in[:, :, D // 2:D], xt[:, :, D // 2:D]).then_inc(x_loaded2, 16)
            for kind, f in stages:
                (hyb_sync if kind == "hyb" else swa_sync)(sp) if kind != "ffn" else ffn_sync(sp, f)
            sp.wait_ge(w_used, first["ffn3"] + 1)
            sp.dma_start(final_g, t["final_norm"].partition_broadcast(P)).then_inc(final_loaded, 16)
            for b in range(TB):
                sp.wait_ge(out_ready, b + 1)
                sp.dma_start(out[b * P:(b + 1) * P, :], y_out[:, b, :]).then_inc(stored, 16)
            sp.wait_ge(stored, 16 * TB)

        @block.gpsimd
        def _(pool):
            nc.gpsimd.memset(ones[:], 1.0).then_inc(set_up, 1)
            nc.gpsimd.memset(zeros[:], 0.0).then_inc(set_up, 1)
            nc.gpsimd.memset(neg_half[:], -0.5).then_inc(set_up, 1)
            mark(nc.gpsimd.memset(wba_pad, 0.0), "wba_cleared")
            pool.wait_ge(set_up, 3)
            for n, (kind, f) in enumerate(stages):
                if kind == "hyb":
                    pool.wait_ge(rest_loaded, 16 * 5)
                    need(pool, "wba_hi")
                    mark(nc.gpsimd.tensor_tensor(wba_lo, wba_pad, wba_hi.bitcast(F32), ALU.subtract), "wba_split")
                if kind == "swa":
                    pool.wait_ge(w_used, first["ffn2"] + 1)
                    mark(nc.gpsimd.memset(work[:, 1536:3072], 0.0), "k_padded")
                norm_pool(pool, n)
                if kind == "ffn":
                    norm_half(pool, n)
                    ffn_pool(pool, f)
                elif kind == "hyb":
                    hyb_pool(pool)
                else:
                    swa_pool(pool)
            pool.wait_ge(fin_step, 1)
            nc.gpsimd.tensor_tensor(fin_r[:], fin_v[:], neg_half[:].to_broadcast([P, TB]), ALU.pow) \
              .then_inc(fin_rstd, 1)


        @block.scalar
        def _(act_e):
            small = [(vec_rows[0:KT, :], t["ffn1_norm"][0]), (vec_rows[KT:2 * KT, :], t["mix_norm"][0]),
                     (vec_rows[2 * KT:3 * KT, :], t["ffn2_norm"][0]), (vec_rows[3 * KT:4 * KT, :], t["ffn1_norm"][1]),
                     (vec_rows[4 * KT:5 * KT, :], t["mix_norm"][1]), (vec_rows[5 * KT:6 * KT, :], t["ffn2_norm"][1]),
                     (vec_rows[V_BO:V_BO + KT, :], t["swa_b_o"][0])]
            for dst, src in small:
                act_e.dma_start(dst, src.rearrange("(k p) -> k p", p=P)).then_inc(vec_loaded, 16)
            act_e.dma_start(vec_rows[V_CONV:V_CONV + 48, :], t["gdn_conv_w"][0].rearrange("w (k p) -> (w k) p", p=P)) \
                 .then_inc(vec_loaded, 16)
            act_e.dma_start(vec_rows[V_SC:V_SC + 12, :], t["sc_conv_w"][0].rearrange("w (k p) -> (w k) p", p=P)) \
                 .then_inc(vec_loaded, 16)
            act_e.dma_start(vec_rows[V_GN:V_GN + 1, :], t["gdn_out_norm"]).then_inc(vec_loaded, 16)
            act_e.wait_ge(vec_ready, 1)
            for n, (kind, f) in enumerate(stages):
                c = first[{"ffn": f"ffn{f}", "hyb": "hyb_in", "swa": "swa_in"}[kind]]
                mixed = n and stages[n - 1][0] != "ffn"
                if kind == "hyb":
                    act_e.wait_ge(rest_loaded, 16 * 5)
                    mark(nc.scalar.activation(wba_hi, wba_pad, ACT.Copy), "wba_hi")
                if n == 0:
                    norm_scalar(act_e, n, lambda j: j == 2 and split_hi(act_e, (0, 0), check=False))
                    split_hi(act_e, (1, 0), check=False)
                    split_hi(act_e, (2, 0), check=False)
                    load_rest(act_e)
                else:
                    norm_scalar(act_e, n, (lambda j: j != 1 and split_hi(act_e, (c - 1 + (j + 1) // 2, 0)))
                                if mixed else None)
                    split_hi(act_e, (c + 2, 0))
                norm_rstd(act_e, n)
                if kind == "ffn":
                    ffn_scalar(act_e, f, n)
                elif kind == "hyb":
                    hyb_scalar(act_e, n)
                else:
                    swa_scalar(act_e, n)
            for b in range(TB):
                if b < TB - 1:
                    act_e.wait_ge(fin_acc, b + 1)
                else:
                    act_e.wait_ge(w_used, CHUNKS)
                for half in range(2):
                    i = nc.scalar.activation(fin_t[:, (2 * b + half) * 512:(2 * b + half + 1) * 512], ACC[2 * b + half][:], ACT.Square,
                                             accum_out=fin_ss[:, b, half:half + 1])
                i.then_inc(fin_sq, 1)

        @block.vector
        def _(dve):
            dve.wait_ge(vec_tr, 1)
            nc.vector.tensor_copy(vecT[:], AUX[:, 0:NVEC]).then_inc(vec_ready, 1)
            dve.wait_ge(vec_ready, 1)
            for n, (kind, f) in enumerate(stages):
                c = first[{"ffn": f"ffn{f}", "hyb": "hyb_in", "swa": "swa_in"}[kind]]
                mixed = n and stages[n - 1][0] != "ffn"
                banks, ready = update(n)
                norm_vector(dve, n, banks, ready,
                            vecT[:, V_BO:V_BO + KT] if n and stages[n - 1][0] == "swa" else None,
                            (lambda k: split_lo(dve, (c - 1 + k, 0), handed_over=(k == 0)))
                            if mixed else
                            (lambda k: k and split_lo(dve, (k - 1, 0))) if n == 0 else None)
                split_lo(dve, (c + 2, 0))
                norm_var(dve, n)
                dve.wait_ge(rstd_ready, n + 1)
                if kind == "ffn":
                    ffn_vector(dve, f, n)
                elif kind == "hyb":
                    hyb_vector(dve, n)
                else:
                    swa_vector(dve, n)
            dve.wait_ge(fin_sq, TB)
            nc.vector.tensor_tensor(fin_v[:], fin_ss[:, :, 0], fin_ss[:, :, 1], ALU.add).then_inc(fin_dve, 1)
            dve.wait_ge(fin_dve, 1)
            nc.vector.tensor_scalar(fin_v[:], fin_v[:], 1.0 / D, EPS, ALU.mult, ALU.add).then_inc(fin_step, 1)
            dve.wait_ge(fin_rstd, 1)
            dve.wait_ge(final_loaded, 16)
            for b in range(TB):
                for half in range(2):
                    cols = slice(half * 512, (half + 1) * 512)
                    i = nc.vector.scalar_tensor_tensor(out=y_out[:, b, cols], in0=ACC[2 * b + half][:],
                                                       scalar=fin_r[:, b:b + 1], in1=final_g[:, cols],
                                                       op0=ALU.mult, op1=ALU.mult)
                i.then_inc(out_ready, 1)


        @block.tensor
        def _(pe):
            pe.wait_ge(x_loaded, 32)
            for j in range(PAIRS):
                if j == PAIRS // 2:
                    pe.wait_ge(vec_loaded, 16 * 10)
                    nc.tensor.transpose(AUX[:, 0:NVEC], vec_rows[:], ident[0:NVEC, 0:NVEC]).then_inc(vec_tr, 1)
                    pe.wait_ge(x_loaded2, 16)
                for kt in (2 * j, 2 * j + 1):
                    for b in range(TB):
                        o = (kt % 2) * SEQ + b * P
                        last = nc.tensor.transpose(ACC[j][:, o:o + P], x_in[:, b, kt * P:(kt + 1) * P], ident)
                last.then_inc(acc_done, 1)
            for n, (kind, f) in enumerate(stages):
                if n == 0:
                    pe.wait_ge(vec_ready, 1)
                    pe.wait_ge(set_up, 3)
                if kind == "ffn":
                    ffn_tensor(pe, f, n)
                elif kind == "hyb":
                    hyb_tensor(pe, n)
                else:
                    swa_tensor(pe, n)


_INS = ["x", "ffn1_norm", "ffn1_w_gate", "ffn1_w_up", "ffn1_w_down", "mix_norm", "ffn2_norm", "ffn2_w_gate",
        "ffn2_w_up", "ffn2_w_down", "hyb_w_in", "gdn_conv_w", "gdn_a_log", "gdn_dt_bias", "gdn_out_norm",
        "sc_conv_w", "hyb_w_out", "swa_w_qkv", "swa_b_qkv", "swa_sinks", "swa_w_o", "swa_b_o", "final_norm"]

MIX = (True, True)


def build(nc, arrays):
    t = {}
    for name, a in arrays.items():
        t[name] = nc.dram_tensor(f"in_{name}", a.shape, F32, kind="ExternalInput").ap()
    out = nc.dram_tensor("out", (256, 1024), F32, kind="ExternalOutput").ap()
    trunk(nc, t, out, MIX)


def kernel(**inputs):
    import numpy as _np
    import concourse.bacc as _bacc
    from concourse.bass_utils import run_bass_kernel_spmd as _run

    nc = _bacc.Bacc("TRN2", target_bir_lowering=False, num_devices=1)
    arrays = {name: _np.ascontiguousarray(inputs[name]) for name in _INS}
    arrays["constants"] = constants()
    build(nc, arrays)
    r = _run(nc, [{f"in_{k}": v for k, v in arrays.items()}], core_ids=[0])
    return r.results[0]["out"].reshape(1, 256, 1024)
```

```python
from contextlib import ExitStack
from itertools import count

import concourse.bass as bass
from concourse import mybir

ALU = mybir.AluOpType
ACT = mybir.ActivationFunctionType
F32 = mybir.dt.float32
F32R = mybir.dt.float32r
AX = mybir.AxisListType

P = 128
RING = 3
CW = 256
MASKED = -1.0e30

K_IDENT = 0
K_TRI = 128
K_BLK = 256
K_LEVEL = 384
N_LEVEL = 6
K_ATT0 = K_LEVEL + N_LEVEL * 128
K_ATT1 = K_ATT0 + 128
K_COS = K_ATT1 + 256
K_SIN = K_COS + 128
K_END = K_SIN + 128


def constants():
    import numpy as np

    t = np.zeros((P, K_END), np.float32)
    s = np.arange(P)[:, None]
    c = np.arange(P)[None, :]
    same = (s // 64) == (c // 64)
    t[:, K_IDENT:K_IDENT + 128] = s == c
    t[:, K_TRI:K_TRI + 128] = same & (s <= c)
    t[:, K_BLK:K_BLK + 128] = same
    for n in range(N_LEVEL):
        b = 1 << n
        t[:, K_LEVEL + 128 * n:K_LEVEL + 128 * (n + 1)] = (
            (s // (2 * b) == c // (2 * b)) & (s % (2 * b) < b) & (c % (2 * b) >= b))
    t[:, K_ATT0:K_ATT0 + 128] = np.where(c <= s, 0.0, MASKED)
    kj = np.arange(256)[None, :]
    t[:, K_ATT1:K_ATT1 + 256] = np.where((kj > s) & (kj <= s + 128), 0.0, MASKED)
    half = 32
    inv = (np.float32(10000.0) ** (-np.arange(half, dtype=np.float32) / np.float32(half))).astype(np.float32)
    ang = np.arange(256, dtype=np.float32)[:, None] * inv[None, :]
    cos, sin = np.cos(ang), np.sin(ang)
    for b in range(2):
        rows = slice(128 * b, 128 * b + 128)
        t[:, K_COS + 64 * b:K_COS + 64 * b + 64] = np.concatenate([cos[rows], cos[rows]], 1)
        t[:, K_SIN + 64 * b:K_SIN + 64 * b + 64] = np.concatenate([-sin[rows], sin[rows]], 1)
    return t


def trunk(nc, t, out):
    SEQ, D = t["x"].shape[1:]
    DEPTH, _, FF = t["ffn1_w_gate"].shape
    KT = D // P
    PAIRS = KT // 2
    TB = SEQ // P
    NG = FF // CW
    HG = CW // P
    FFN_CHUNKS = 3 * NG
    EPS = 1e-6
    assert (SEQ, D, DEPTH) == (256, 1024, 2) and FF == NG * CW

    HYB_IN, HYB_OUT = 14, D // CW
    SWA_IN, SWA_OUT = 6, D // CW
    first = {}
    at = 0
    for name, n in (("ffn0", FFN_CHUNKS), ("hyb_in", HYB_IN), ("hyb_out", HYB_OUT), ("ffn1", FFN_CHUNKS),
                    ("ffn2", FFN_CHUNKS), ("swa_in", SWA_IN), ("swa_out", SWA_OUT), ("ffn3", FFN_CHUNKS)):
        first[name] = at
        at += n
    CHUNKS = at
    ffn_w = [("ffn1", 0), ("ffn2", 0), ("ffn1", 1), ("ffn2", 1)]

    with ExitStack() as ctx:
        def sb(name, shape, dt=F32):
            return ctx.enter_context(nc.sbuf_tensor(name, shape, dt))

        def sem(name):
            return ctx.enter_context(nc.semaphore(name))

        raw = sb("raw", [P, RING, 2048])
        w_hi = [sb(f"w_hi{n}", [P, 2048], F32R) for n in range(RING)]
        w_lo = [sb(f"w_lo{n}", [P, 2048], F32R) for n in range(RING)]
        kon = sb("kon", [P, K_END])
        ident = kon[:, K_IDENT:K_IDENT + P]
        ones = sb("ones", [P, P])
        xT = sb("xT", [P, KT, SEQ])
        h_hi = sb("h_hi", [P, KT, SEQ], F32R)
        h_lo = sb("h_lo", [P, KT, SEQ], F32R)
        m_hi = sb("m_hi", [P, KT, SEQ], F32R)
        m_lo = sb("m_lo", [P, KT, SEQ], F32R)
        last_hi, last_lo = m_hi[:, 6:8, :], m_lo[:, 6:8, :]
        sq = sb("sq", [P, PAIRS, 2 * SEQ])
        var = sb("var", [P, SEQ + TB])
        rstd = sb("rstd", [P, SEQ + TB])
        neg_half = sb("neg_half", [P, 1])
        gate = sb("gate", [P, 2 * SEQ])
        silu = sb("silu", [P, 2 * SEQ])
        silu_r = sb("silu_r", [P, 2 * SEQ])
        act = sb("act", [P, 2 * SEQ])
        act_hi = sb("act_hi", [P, 2, SEQ], F32R)
        act_lo = sb("act_lo", [P, 2, SEQ], F32R)
        NVEC = 7 * KT + 48 + 12 + 1
        FIRST_VEC = DEPTH * KT
        vecT = sb("vecT", [P, NVEC])
        V_NORM, V_CONV, V_SC, V_GN, V_BO = 0, 6 * KT, 6 * KT + 48, 6 * KT + 60, 6 * KT + 61

        def norm_column(n):
            return V_NORM + (n % 3) * DEPTH * KT + (n // 3) * KT

        work = sb("work", [P, 16 * 1024])
        rstd_half = work[:, 15 * 1024:15 * 1024 + SEQ]
        vec_rows = work[0:NVEC, 14 * 1024:14 * 1024 + P]

        fin_ss = sb("fin_ss", [P, TB, 2])
        fin_v = sb("fin_v", [P, TB])
        fin_r = sb("fin_r", [P, TB])
        bank = [ctx.enter_context(nc.psum_tensor(f"bank{n}", [P, 512], F32)) for n in range(8)]
        GATE, UP, ACC, AUX, AUX2 = bank[0], bank[1], bank[2:6], bank[6], bank[7]
        OUT_BANKS = [GATE, UP, AUX, AUX2]

        w_loaded = [sem(f"w_loaded{n}") for n in range(RING)]
        hi_split = sem("hi_split")
        lo_split = sem("lo_split")
        w_used = sem("w_used")
        ident_loaded = sem("ident_loaded")
        x_loaded = sem("x_loaded")
        x_loaded2 = sem("x_loaded2")
        first_vec_loaded = sem("first_vec_loaded")
        vec_loaded = sem("vec_loaded")
        rest_loaded = sem("rest_loaded")
        bias_loaded = sem("bias_loaded")
        final_loaded = sem("final_loaded")
        stored = sem("stored")
        set_up = sem("set_up")
        wba_cleared = sem("wba_cleared")
        first_half_loaded = sem("first_half_loaded")
        first_half_split = sem("first_half_split")
        vec_turned = sem("vec_turned")
        vec_ready = sem("vec_ready")
        acc_done = sem("acc_done")
        x_updated = sem("x_updated")
        sq_ready = sem("sq_ready")
        sq_step = sem("sq_step")
        sq_summed = sem("sq_summed")
        ss_ready = sem("ss_ready")
        var_step = sem("var_step")
        var_ready = sem("var_ready")
        rstd_ready = sem("rstd_ready")
        half_ready = sem("half_ready")
        h_hi_ready = sem("h_hi_ready")
        h_ready = sem("h_ready")
        gate_read = sem("gate_read")
        silu_ready = sem("silu_ready")
        silu_r_ready = sem("silu_r_ready")
        up_read = sem("up_read")
        act_hi_ready = sem("act_hi_ready")
        act_ready = sem("act_ready")
        fin_acc = sem("fin_acc")
        fin_sq = sem("fin_sq")
        fin_sum = sem("fin_sum")
        fin_var = sem("fin_var")
        fin_rstd = sem("fin_rstd")
        out_ready = sem("out_ready")
        vector_step = sem("vector_step")
        steps = count(1)
        hyb_evacuated = sem("hyb_evacuated")
        wba_hi_ready = sem("wba_hi_ready")
        wba_split = sem("wba_split")
        gates_projected = sem("gates_projected")
        gates_scaled = sem("gates_scaled")
        gates_turned = sem("gates_turned")
        minus_abs = sem("minus_abs")
        gates_exp = sem("gates_exp")
        log_ready = sem("log_ready")
        g_ready = sem("g_ready")
        g_summed = sem("g_summed")
        g_copied = sem("g_copied")
        kq_silu = sem("kq_silu")
        v_silu = sem("v_silu")
        kq_turned = sem("kq_turned")
        kq_squared = sem("kq_squared")
        norms_inverted = sem("norms_inverted")
        norms_rooted = sem("norms_rooted")
        gates_raised = sem("gates_raised")
        diagonals_ready = sem("diagonals_ready")
        rows_summed = sem("rows_summed")
        decay_arg = sem("decay_arg")
        rows_exp = sem("rows_exp")
        decay_ready = sem("decay_ready")
        kq_scaled = sem("kq_scaled")
        kq_turned_back = sem("kq_turned_back")
        kq_copied = sem("kq_copied")
        k_scaled = sem("k_scaled")
        qg_ready = sem("qg_ready")
        pair_products = sem("pair_products")
        pairs_masked = sem("pairs_masked")
        inverse_t_ready = sem("inverse_t_ready")
        inverse_turned = sem("inverse_turned")
        inverse_ready = sem("inverse_ready")
        level_masked = sem("level_masked")
        left_done = sem("left_done")
        left_copied = sem("left_copied")
        right_done = sem("right_done")
        v_turned = sem("v_turned")
        v_scaled = sem("v_scaled")
        solved = sem("solved")
        solutions_copied = sem("solutions_copied")
        state_read = sem("state_read")
        v_new_ready = sem("v_new_ready")
        state_added = sem("state_added")
        state_ready = sem("state_ready")
        o_ready = sem("o_ready")
        o_squared = sem("o_squared")
        o_summed = sem("o_summed")
        o_inverted = sem("o_inverted")
        o_rooted = sem("o_rooted")
        o_diagonal = sem("o_diagonal")
        o_rows_ready = sem("o_rows_ready")
        z_silu = sem("z_silu")
        z_weighted = sem("z_weighted")
        o_gate_done = sem("o_gate_done")
        o_final = sem("o_final")
        o_hi_ready = sem("o_hi_ready")
        o_split = sem("o_split")
        sc_conv_done = sem("sc_conv_done")
        conv_gated = sem("conv_gated")
        conv_hi_ready = sem("conv_hi_ready")
        conv_split = sem("conv_split")
        conv_done = {x: sem(f"conv_{x}_done") for x in "kqv"}
        swa_evacuated = sem("swa_evacuated")
        k_padded = sem("k_padded")
        x_cos_ready = sem("x_cos_ready")
        k_rotated = sem("k_rotated")
        q_rotated = sem("q_rotated")
        k_transposed = sem("k_transposed")
        k_copied = sem("k_copied")
        q_transposed = sem("q_transposed")
        q_copied = sem("q_copied")
        scores_ready = sem("scores_ready")
        scores_read = sem("scores_read")
        max_ready = sem("max_ready")
        probs_ready = sem("probs_ready")
        probs_transposed = sem("probs_transposed")
        prob_copied = sem("prob_copied")
        den_ready = sem("den_ready")
        values_summed = sem("values_summed")
        o_normed = sem("o_normed")
        o_transposed = sem("o_transposed")
        o_hi_done = sem("o_hi_done")
        o_lo_done = sem("o_lo_done")

        def number(ch):
            return ch[0] + RING * ch[1]

        def slot(ch):
            return ch[0] % RING

        def load(sp, ch, src, check=True):
            if check:
                sp.wait_ge(lo_split, number(ch) - RING + 1)
            n = src.shape[1]
            sp.dma_start(raw[:, slot(ch), :].rearrange("p (a b) -> p a b", a=n), src) \
              .then_inc(w_loaded[slot(ch)], 16)

        def split_hi(act_e, ch, check=True):
            act_e.wait_ge(w_loaded[slot(ch)], 16 * (ch[0] // RING + 1 + ch[1]))
            if check:
                act_e.wait_ge(w_used, number(ch) - RING + 1)
            nc.scalar.activation(w_hi[slot(ch)][:], raw[:, slot(ch), :], ACT.Copy).then_inc(hi_split, 1)

        def first_split(act_e, half):
            act_e.wait_ge((first_half_loaded, w_loaded[0])[half], 16)
            cols = slice(half * 1024, (half + 1) * 1024)
            nc.scalar.activation(w_hi[0][:, cols], raw[:, 0, cols], ACT.Copy) \
              .then_inc((first_half_split, hi_split)[half], 1)

        def split_lo(eng, ch, by=nc.vector, handed_over=False):
            eng.wait_ge(hi_split, number(ch) + 1)
            if handed_over:
                eng.wait_ge(lo_split, number(ch))
            by.tensor_tensor(w_lo[slot(ch)][:], raw[:, slot(ch), :], w_hi[slot(ch)][:].bitcast(F32),
                             ALU.subtract).then_inc(lo_split, 1)

        def product(out_ap, s, wcols, mv_hi, mv_lo, start, stop=False, part=None):
            if part != 1:
                nc.tensor.matmul(out_ap, w_hi[s][:, wcols], mv_hi, start=start, stop=False, skip_group_check=True)
                i = nc.tensor.matmul(out_ap, w_hi[s][:, wcols], mv_lo, start=False, stop=False,
                                     skip_group_check=True)
            if part == 0:
                return i
            return nc.tensor.matmul(out_ap, w_lo[s][:, wcols], mv_hi, start=False, stop=stop,
                                    skip_group_check=True)

        def column_chunk(pe, ch, dst, m_hi, m_lo, pairs_ready=None, between=None):
            def step(kt, ft, start, stop, part=None):
                return product(dst[:, ft * SEQ:(ft + 1) * SEQ], slot(ch),
                               slice(kt * CW + ft * P, kt * CW + (ft + 1) * P),
                               m_hi[:, kt, :], m_lo[:, kt, :], start=start, stop=stop, part=part)

            if pairs_ready is not None:
                first_chunk = number(ch) == 0
                pe.wait_ge(*((first_half_split, 1) if first_chunk else (hi_split, number(ch) + 1)))
                for kt in range(KT):
                    if first_chunk and kt == KT // 2:
                        pe.wait_ge(hi_split, 1)
                    if kt % 2 == 0:
                        pe.wait_ge(pairs_ready[0], pairs_ready[1] + kt // 2 + 1)
                    for ft in range(HG):
                        step(kt, ft, kt + ft == 0, False, 0)
                pe.wait_ge(lo_split, number(ch) + 1)
                for ft in range(HG):
                    for kt in range(KT):
                        last = step(kt, ft, False, kt == KT - 1, 1)
            else:
                pe.wait_ge(lo_split, number(ch) + 1)
                for ft in range(HG):
                    if between is not None and ft == 1:
                        between()
                    for kt in range(KT):
                        last = step(kt, ft, kt + ft == 0, kt == KT - 1)
            last.then_inc(w_used, 1)

        def norm_ss(pe, n, columns=False):
            pe.wait_ge(sq_summed, n + 1)
            if n:
                pe.wait_ge(var_ready, n)
            last = nc.tensor.matmul(AUX[:, 0:SEQ], ones[:], sq[:, 0, 0:SEQ], start=True, stop=True)
            for b in range(TB if columns else 0):
                last = nc.tensor.matmul(AUX[:, SEQ + b:SEQ + b + 1], sq[:, 0, b * P:(b + 1) * P], ones[:, 0:1],
                                        start=True, stop=True)
            last.then_inc(ss_ready, 1)

        def norm_scalar(act_e, n, before_pair=None):
            for j in range(PAIRS):
                if before_pair is not None:
                    before_pair(j)
                act_e.wait_ge(x_updated, PAIRS * n + j + 1)
                if n:
                    act_e.wait_ge(sq_summed, n)
                    act_e.wait_ge(ss_ready, n)
                for kt in (2 * j, 2 * j + 1):
                    g = norm_column(n) + kt
                    i = nc.scalar.activation(h_hi[:, kt, :], xT[:, kt, :], ACT.Copy, scale=vecT[:, g:g + 1])
                i.then_inc(h_hi_ready, 1)
                if n:
                    nc.scalar.activation(sq[:, j, :], xT[:, 2 * j:2 * j + 2, :].rearrange("p a b -> p (a b)"),
                                         ACT.Square).then_inc(sq_ready, 1)

        def norm_lo(dve, n, j):
            dve.wait_ge(h_hi_ready, PAIRS * n + j + 1)
            for kt in (2 * j, 2 * j + 1):
                g = norm_column(n) + kt
                i = nc.vector.scalar_tensor_tensor(out=h_lo[:, kt, :], in0=xT[:, kt, :], scalar=vecT[:, g:g + 1],
                                                   in1=h_hi[:, kt, :].bitcast(F32), op0=ALU.mult,
                                                   op1=ALU.subtract)
            i.then_inc(h_ready, 1)

        def norm_vector(dve, n, banks, ready, bias=None, early_split=None):
            for j in range(PAIRS):
                dve.wait_ge(*ready[j])
                pair = xT[:, 2 * j:2 * j + 2, :].rearrange("p a b -> p (a b)")
                if n == 0:
                    nc.vector.tensor_copy(pair, banks[j][:]).then_inc(x_updated, 1)
                elif bias is None:
                    nc.vector.tensor_tensor(pair, banks[j][:], pair, ALU.add).then_inc(x_updated, 1)
                else:
                    for kt in (2 * j, 2 * j + 1):
                        i = nc.vector.scalar_tensor_tensor(
                            out=xT[:, kt, :], in0=banks[j][:, (kt % 2) * SEQ:(kt % 2 + 1) * SEQ],
                            scalar=bias[:, kt:kt + 1], in1=xT[:, kt, :], op0=ALU.add, op1=ALU.add)
                    i.then_inc(x_updated, 1)
                if early_split is not None and j == 1:
                    split_lo(dve, early_split, handed_over=True)
                if j:
                    norm_lo(dve, n, j - 1)
            norm_lo(dve, n, PAIRS - 1)

        def norm_pool(pool, n):
            def square(j):
                pool.wait_ge(x_updated, j + 1)
                x = xT[:, 2 * j:2 * j + 2, :].rearrange("p a b -> p (a b)")
                nc.gpsimd.tensor_tensor(sq[:, j, :], x, x, ALU.mult).then_inc(sq_ready, 1)

            if n == 0:
                square(0)
            for j in range(1, PAIRS):
                if n == 0:
                    square(j)
                if j == 1 and n and stages[n - 1][0] != "ffn":
                    split_lo(pool, (first["ffn%d" % stages[n][1]], 0), nc.gpsimd, handed_over=True)
                pool.wait_ge(sq_ready, PAIRS * n + j + 1)
                if j > 1:
                    pool.wait_ge(sq_step, 3 * n + j - 1)
                i = nc.gpsimd.tensor_tensor(sq[:, 0, :], sq[:, 0, :], sq[:, j, :], ALU.add)
                i.then_inc(sq_step, 1)
            pool.wait_ge(sq_step, 3 * (n + 1))
            nc.gpsimd.tensor_tensor(sq[:, 0, 0:SEQ], sq[:, 0, 0:SEQ], sq[:, 0, SEQ:2 * SEQ], ALU.add) \
              .then_inc(sq_summed, 1)


        def norm_var(dve, n):
            dve.wait_ge(ss_ready, n + 1)
            part = var[:, 0:SEQ + (TB if stages[n][0] == "swa" else 0)]
            nc.vector.tensor_scalar(part, AUX[:, 0:part.shape[1]], 1.0 / D, EPS, ALU.mult, ALU.add) \
              .then_inc(var_step, 1)
            dve.wait_ge(var_step, n + 1)
            nc.vector.reciprocal(part, part).then_inc(var_ready, 1)

        def norm_rstd(act_e, n):
            act_e.wait_ge(var_ready, n + 1)
            cols = slice(0, SEQ + (TB if stages[n][0] == "swa" else 0))
            nc.scalar.activation(rstd[:, cols], var[:, cols], ACT.Sqrt).then_inc(rstd_ready, 1)

        def norm_half(pool, n):
            pool.wait_ge(rstd_ready, n + 1)
            nc.gpsimd.tensor_scalar(rstd_half[:], rstd[:, 0:SEQ], 0.5, None, ALU.mult).then_inc(half_ready, 1)
            pool.wait_ge(half_ready, halves_before(n) + 1)

        def halves_before(n):
            return sum(kind == "ffn" for kind, f in stages[:n])

        def over_rows(row, tiles):
            return row.rearrange("p (a s) -> p a s", a=1).to_broadcast([P, tiles, SEQ])

        def ffn_sources(f):
            kind, li = ffn_w[f]
            wg = t[kind + "_w_gate"][li].rearrange("(k p) f -> p k f", p=P)
            wu = t[kind + "_w_up"][li].rearrange("(k p) f -> p k f", p=P)
            wd = t[kind + "_w_down"][li].rearrange("(g k p) d -> g p k d", p=P, k=HG)
            return wg, wu, wd

        def ffn_sync(sp, f):
            c0 = first[f"ffn{f}"]
            wg, wu, wd = ffn_sources(f)
            if f == 0:
                for half, done in enumerate((first_half_loaded, w_loaded[0])):
                    kts = slice(half * KT // 2, (half + 1) * KT // 2)
                    sp.dma_start(raw[:, 0, half * 1024:(half + 1) * 1024].rearrange("p (a b) -> p a b", b=CW),
                                 wg[:, kts, 0:CW]).then_inc(done, 16)
            else:
                load(sp, (c0, 0), wg[:, :, 0:CW])
            load(sp, (c0 + 1, 0), wu[:, :, 0:CW], check=c0 >= RING)

            def group(i):
                cols = bass.ds((i + 1) * CW, CW)
                load(sp, (c0 + 2, i), wg[:, :, cols], check=not isinstance(i, int) or i > 0 or c0 >= RING)
                load(sp, (c0 + 3, i), wu[:, :, cols])
                load(sp, (c0 + 4, i), wd[i])

            group(0)
            with sp.Fori(1, NG - 1) as i:
                group(i)
            load(sp, (c0 + FFN_CHUNKS - 1, 0), wd[NG - 1])

        def ffn_scalar(act_e, f, n):
            c0 = first[f"ffn{f}"]

            def gate_step(g):
                act_e.wait_ge(gate_read, NG * f + g + 1)
                if not isinstance(g, int) or g + f:
                    act_e.wait_ge(silu_r_ready, NG * f + g)
                nc.scalar.activation(silu[:], gate[:], ACT.Silu).then_inc(silu_ready, 1)

            def next_split(ch, last_group=False):
                if not last_group or ch[0] + RING * (ch[1] + 1) < CHUNKS:
                    split_hi(act_e, (ch[0] + RING, ch[1]))

            def act_step(g):
                act_e.wait_ge(up_read, NG * f + g + 1)
                hi = last_hi if isinstance(g, int) and g == NG - 1 else act_hi[:]
                nc.scalar.activation(hi.rearrange("p a b -> p (a b)"), act[:], ACT.Copy) \
                  .then_inc(act_hi_ready, 1)

            gate_step(0)
            next_split((c0, 0))
            next_split((c0 + 1, 0))
            act_step(0)

            def group(i, last_group):
                gate_step(i + 1)
                next_split((c0 + 2, i), last_group)
                next_split((c0 + 3, i), last_group)
                if last_group:
                    act_step(i + 1)
                else:
                    act_e.wait_ge(w_used, number((c0 + 4, i)) + 1)
                    act_step(i + 1)
                next_split((c0 + 4, i), last_group)

            with act_e.Fori(0, NG - 2) as i:
                group(i, False)
            group(NG - 2, True)

        def ffn_vector(dve, f, n):
            c0 = first[f"ffn{f}"]

            def gate_step(g, ch):
                dve.wait_ge(w_used, number(ch) + 1)
                if not isinstance(g, int) or g + f:
                    dve.wait_ge(silu_ready, NG * f + g)
                nc.vector.tensor_tensor(gate[:].rearrange("p (a s) -> p a s", a=2),
                                        GATE[:].rearrange("p (a s) -> p a s", a=2),
                                        over_rows(rstd[:, 0:SEQ], 2), ALU.mult).then_inc(gate_read, 1)

            def up_step(g, ch):
                dve.wait_ge(w_used, number(ch) + 1)
                dve.wait_ge(silu_r_ready, NG * f + g + 1)
                nc.vector.tensor_tensor(act[:], UP[:], silu_r[:], ALU.mult).then_inc(up_read, 1)

            def lo_step(g):
                dve.wait_ge(act_hi_ready, NG * f + g + 1)
                hi, lo = (last_hi, last_lo) if isinstance(g, int) and g == NG - 1 else (act_hi[:], act_lo[:])
                nc.vector.tensor_tensor(lo.rearrange("p a b -> p (a b)"), act[:],
                                        hi.rearrange("p a b -> p (a b)").bitcast(F32),
                                        ALU.subtract).then_inc(act_ready, 1)

            def next_split(ch, last_group=False):
                if not last_group or ch[0] + RING * (ch[1] + 1) < CHUNKS:
                    split_lo(dve, (ch[0] + RING, ch[1]))

            gate_step(0, (c0, 0))
            if f == 0:
                dve.wait_ge(vec_turned, 2)
                nc.vector.tensor_copy(vecT[:, FIRST_VEC:NVEC], AUX2[:, FIRST_VEC:NVEC]).then_inc(vec_ready, 1)
            next_split((c0, 0))
            up_step(0, (c0 + 1, 0))
            next_split((c0 + 1, 0))
            lo_step(0)

            def group(i, last_group):
                gate_step(i + 1, (c0 + 2, i))
                next_split((c0 + 2, i), last_group)
                up_step(i + 1, (c0 + 3, i))
                next_split((c0 + 3, i), last_group)
                lo_step(i + 1)
                if not last_group:
                    next_split((c0 + 4, i))

            with dve.Fori(0, NG - 2) as i:
                group(i, False)
            group(NG - 2, True)

        def ffn_pool(pool, f):
            with pool.Fori(0, NG) as g:
                pool.wait_ge(silu_ready, g + (NG * f + 1))
                nc.gpsimd.tensor_tensor(silu_r[:].rearrange("p (a s) -> p a s", a=2),
                                        silu[:].rearrange("p (a s) -> p a s", a=2),
                                        over_rows(rstd_half[:], 2), ALU.mult).then_inc(silu_r_ready, 1)

        def ffn_tensor(pe, f, n):
            c0 = first[f"ffn{f}"]
            final = f == 3

            def gate_chunk(g, ch, pairs_ready=None):
                column_chunk(pe, ch, GATE, h_hi, h_lo, pairs_ready)

            def down_chunk(ch, g, done=None, opens=False):
                pe.wait_ge(lo_split, number(ch) + 1)
                pe.wait_ge(act_ready, NG * f + g + 1)
                s = slot(ch)
                a_hi, a_lo = (last_hi, last_lo) if isinstance(g, int) and g == NG - 1 else (act_hi[:], act_lo[:])
                if final:
                    for b in range(TB):
                        for half in range(2):
                            for k in range(HG):
                                tok = slice(b * P, (b + 1) * P)
                                cols = slice(k * D + half * 512, k * D + (half + 1) * 512)
                                o = ACC[2 * b + half][:]
                                for st, mv in ((a_hi, w_hi), (a_lo, w_hi), (a_hi, w_lo)):
                                    last = nc.tensor.matmul(o, st[:, k, tok], mv[s][:, cols], start=False,
                                                            stop=False, skip_group_check=True)
                            if done is not None and (b, half) != (TB - 1, 1):
                                last.then_inc(done, 1)
                else:
                    for dt in range(KT):
                        for k in range(HG):
                            last = product(ACC[dt // 2][:, (dt % 2) * SEQ:(dt % 2 + 1) * SEQ], s,
                                           slice(k * D + dt * P, k * D + (dt + 1) * P),
                                           a_hi[:, k, :], a_lo[:, k, :], start=(opens and dt % 2 + k == 0))
                        if done is not None and dt % 2 and dt < KT - 1:
                            last.then_inc(done, 1)
                last.then_inc(w_used, 1)

            gate_chunk(0, (c0, 0), (h_ready, PAIRS * n))
            norm_ss(pe, n)
            column_chunk(pe, (c0 + 1, 0), UP, h_hi, h_lo)
            if f == 0:
                pe.wait_ge(vec_loaded, 16 * 6)
                nc.tensor.transpose(AUX2[:, 0:NVEC], vec_rows[:], ident[0:NVEC, 0:NVEC]).then_inc(vec_turned, 1)
            if final:
                for b in range(TB):
                    for kt in range(KT):
                        nc.tensor.matmul(ACC[2 * b + kt // 4][:, (kt % 4) * P:(kt % 4 + 1) * P],
                                         xT[:, kt, b * P:(b + 1) * P], ident, start=(kt % 4 == 0), stop=False,
                                         skip_group_check=True)

            def group(i):
                pe.wait_ge(gate_read, i + (NG * f + 1))
                gate_chunk(None, (c0 + 2, i))
                pe.wait_ge(up_read, i + (NG * f + 1))
                column_chunk(pe, (c0 + 3, i), UP, h_hi, h_lo)
                down_chunk((c0 + 4, i), i, opens=(isinstance(i, int) and i == 0 and not final))

            group(0)
            with pe.Fori(1, NG - 1) as i:
                group(i)
            down_chunk((c0 + FFN_CHUNKS - 1, 0), NG - 1, done=fin_acc if final else acc_done)

        fin_t = work[:, 2048:4096]
        final_g = work[:, 4096:4096 + D]
        x_in = work[:, 0:TB * D].rearrange("p (b d) -> p b d", b=TB)
        y_out = work[:, 0:TB * D].rearrange("p (b d) -> p b d", b=TB)

        KEY = 512
        HEADS = 4
        DK = KEY // HEADS
        SCC = 4 * KEY + 2 * HEADS
        HYB_COLS = [KEY, KEY + CW, 0, CW, SCC + 512, SCC + 512 + CW, 2 * KEY, 2 * KEY + CW, SCC + 1024,
                    SCC + 1024 + CW, SCC, SCC + CW, 3 * KEY, 3 * KEY + CW]
        KINDS = "kqcvhbz"
        CHUNK = 64
        JC = P // CHUNK
        NS = TB * HEADS

        def room(k, n=1):
            return work[:, k * 1024:(k + n) * 1024]

        def by_tile(ap):
            return ap.rearrange("p (h s) -> p h s", s=SEQ)

        def by_pair(ap, b):
            return ap.rearrange("p (b h s) -> p b h s", b=TB, h=HEADS)[:, b]

        def one(ap, b, h):
            n = b * HEADS + h
            return ap[:, n * P:(n + 1) * P]

        def bank_pair(bk):
            return bk[:].rearrange("p (h s) -> p h s", h=HEADS)

        def spread(cols, b):
            return cols[:, b * HEADS:(b + 1) * HEADS].rearrange("p (h s) -> p h s", s=1) \
                .to_broadcast([P, HEADS, P])

        def wide(cols):
            return cols.rearrange("p (n s) -> p n s", s=1).to_broadcast([P, NS, P])

        def table(col, n):
            return kon[:, col:col + P].rearrange("p (a s) -> p a s", a=1).to_broadcast([P, n, P])

        def cube(ap):
            return ap.rearrange("p (n s) -> p n s", s=P)

        k_t, q_t, v_t = room(0), room(1), room(2)
        z_t = room(3)
        conv_in = {"k": room(5), "q": room(6), "v": room(7)}
        conv_out = {"k": k_t, "q": q_t, "v": v_t}
        sc_c, sc_conv = room(8), room(11)
        sc_u, sc_tmp, y_sc = sc_c, (gate, silu), sc_conv
        g_diag = room(5)
        kb_tok, qs_tok = room(6), room(4)
        g_exp = room(12)
        decay = room(10)
        kb_t, qs_t, qg_t = room(3), room(11), room(4)
        lower, attn = room(9), room(5)
        kb_g, k_g, v_b = room(14), room(13), room(10)
        step_m = [room(6), room(1)]
        inv, inv_t = room(0), room(15)
        prod = sq[:, 0:2, :].rearrange("p a b -> p (a b)")
        u_sol, w_sol = room(6), room(2)
        state = [room(0)[:, 0:512], room(0)[:, 512:1024]]
        v_new = [room(1)[:, 0:512], room(1)[:, 512:1024]]
        o_gated, o_diag = room(8), room(9)

        tiny = sb("tiny", [P, 24, NS])
        (T_B, T_A, T_NEG, T_U, T_W, T_D, T_R, T_LN, T_G, T_EB, T_BETA, T_GC, T_GL, T_EGC, T_EKG, T_RK, T_RQ,
         T_R1, T_F1, T_F2, T_OS, T_Y, T_X, T_RO) = range(24)

        def ty(k):
            return tiny[:, k, :]

        wba_pad = room(13)
        wba_hi = m_hi[:, 0:4, :].rearrange("p a b -> p (a b)")
        wba_lo = m_lo[:, 0:4, :].rearrange("p a b -> p (a b)")
        ba_row = act[:, 0:SEQ]
        gate_par = sb("gate_par", [P, 3, HEADS])

        def hyb_sync(sp):
            w = t["hyb_w_in"][0].rearrange("(k p) f -> p k f", p=P)
            for m in range(HYB_IN):
                load(sp, (first["hyb_in"] + m, 0), w[:, :, HYB_COLS[m]:HYB_COLS[m] + CW])
            w = t["hyb_w_out"][0].rearrange("(k p) f -> p k f", p=P)
            for m in range(HYB_OUT):
                load(sp, (first["hyb_out"] + m, 0), w[:, :, m * CW:(m + 1) * CW])

        HYB_PLAN = {(0, 1): ["gates"], (1, 1): ["gates_turned"], (3, 1): ["gates_logged"], (4, 1): ["scalars"],
                    (5, 1): ["rows"], (6, 1): ["products"], (7, 0): ["start"]}
        spots = [(7, 1)] + [(m, half) for m in range(8, HYB_IN) for half in range(2)]
        phases = [f"{x}{n}" for n in range(1, N_LEVEL) for x in ("left", "right")] + ["solutions", "add0", "read1"]
        for spot, name in zip(spots, phases):
            HYB_PLAN[spot] = [name]
        assert len(phases) == len(spots)
        LAST_STEP = TB * JC - 1

        def hyb_tensor_phase(pe, name):
            mm = nc.tensor.matmul
            if name == "gates":
                pe.wait_ge(wba_split, 1)
                for kt in range(KT):
                    cols = slice(kt * P, (kt + 1) * P)
                    mm(AUX2[:, 0:SEQ], wba_hi[:, cols], h_hi[:, kt, :], start=(kt == 0), stop=False)
                    mm(AUX2[:, 0:SEQ], wba_hi[:, cols], h_lo[:, kt, :], start=False, stop=False)
                    i = mm(AUX2[:, 0:SEQ], wba_lo[:, cols], h_hi[:, kt, :], start=False, stop=(kt == KT - 1))
                i.then_inc(gates_projected, 1)
            if name == "gates_turned":
                pe.wait_ge(gates_scaled, 1)
                for b in range(TB):
                    i = nc.tensor.transpose(AUX2[:, b * P:(b + 1) * P], ba_row[:, b * P:(b + 1) * P], ident)
                i.then_inc(gates_turned, 1)
            if name == "scalars":
                pe.wait_ge(kq_silu, 4)
                for which, src in enumerate((k_t, q_t)):
                    for b in range(TB):
                        for h in range(HEADS):
                            i = nc.tensor.transpose(ACC[2 * which + b][:, h * P:(h + 1) * P],
                                                    by_tile(src)[:, h, b * P:(b + 1) * P], ident)
                i.then_inc(kq_turned, 1)
                pe.wait_ge(g_ready, 1)
                mm(AUX2[:, 16:24], kon[:, K_TRI:K_TRI + P], ty(T_G), start=True, stop=True)
                i = mm(AUX2[:, 24:32], kon[:, K_BLK:K_BLK + P], ty(T_G), start=True, stop=True)
                i.then_inc(g_summed, 1)
                pe.wait_ge(diagonals_ready, 1)
                pe.wait_ge(g_copied, 1)
                for n, bk in enumerate((AUX, AUX2)):
                    i = mm(bk[:], ones[:], g_diag[:, n * 512:(n + 1) * 512], start=True, stop=True)
                i.then_inc(rows_summed, 1)
            if name == "rows":
                for k, (src, banks) in enumerate(((qs_tok, ACC[2:4]), (kb_tok, (AUX, AUX2)))):
                    pe.wait_ge(kq_scaled, k + 1)
                    if k == 1:
                        pe.wait_ge(decay_arg, 1)
                        pe.wait_ge(rows_exp, 3)
                    for b in range(TB):
                        for h in range(HEADS):
                            i = nc.tensor.transpose(banks[b][:, h * P:(h + 1) * P], one(src, b, h), ident)
                    i.then_inc(kq_turned_back, 1)
            if name == "products":
                for k, (rhs, banks) in enumerate(((kb_t, (AUX, AUX2)), (qs_t, ACC[2:4]))):
                    pe.wait_ge(kq_copied, 2 - k)
                    for b in range(TB):
                        for h in range(HEADS):
                            i = mm(banks[b][:, h * P:(h + 1) * P], by_tile(k_t)[:, h, b * P:(b + 1) * P],
                                   one(rhs, b, h), start=True, stop=True)
                    i.then_inc(pair_products, 1)
            if name == "start":
                pe.wait_ge(pairs_masked, 1)
                pe.wait_ge(inverse_t_ready, 1)
                for b in range(TB):
                    for h in range(HEADS):
                        i = nc.tensor.transpose((AUX, AUX2)[b][:, h * P:(h + 1) * P], one(inv_t, b, h), ident)
                i.then_inc(inverse_turned, 1)
            if name[:4] == "left":
                n = int(name[4:])
                pe.wait_ge(level_masked, n)
                pe.wait_ge(inverse_ready, n)
                for b in range(TB):
                    for h in range(HEADS):
                        i = mm((AUX, AUX2)[b][:, h * P:(h + 1) * P], one(step_m[n % 2], b, h), one(inv, b, h),
                               start=True, stop=True)
                    i.then_inc(left_done, 1)
            if name[:5] == "right":
                n = int(name[5:])
                if n == N_LEVEL - 1:
                    pe.wait_ge(v_silu, 2)
                    for b in range(TB):
                        for h in range(HEADS):
                            i = nc.tensor.transpose(ACC[2 + b][:, h * P:(h + 1) * P],
                                                    by_tile(v_t)[:, h, b * P:(b + 1) * P], ident)
                    i.then_inc(v_turned, 1)
                for b in range(TB):
                    pe.wait_ge(left_copied, TB * (n - 1) + b + 1)
                    if b == 0:
                        pe.wait_ge(inverse_t_ready, n)
                        pe.wait_ge(k_scaled, 2)
                        pe.wait_ge(pairs_masked, 2)
                    for h in range(HEADS):
                        i = mm(ACC[b][:, h * P:(h + 1) * P], one(prod, b, h), one(inv_t, b, h), start=True,
                               stop=True)
                    if n < N_LEVEL - 1:
                        for h in range(HEADS):
                            i = mm(ACC[2 + b][:, h * P:(h + 1) * P], one(inv_t, b, h), one(prod, b, h),
                                   start=True, stop=True)
                    i.then_inc(right_done, 1)
            if name[:4] == "read":
                s = int(name[4:])
                b, j = divmod(s, JC)
                rows = slice(j * CHUNK, (j + 1) * CHUNK)
                pe.wait_ge(solutions_copied, 2)
                pe.wait_ge(state_ready, s)
                for h in range(HEADS):
                    i = mm(ACC[0][rows, h * P:(h + 1) * P], one(w_sol, b, h)[:, rows],
                           state[s % 2][:, h * P:(h + 1) * P], start=True, stop=True)
                i.then_inc(state_read, 1)
            if name[:3] == "add":
                s = int(name[3:])
                b, j = divmod(s, JC)
                rows = slice(j * CHUNK, (j + 1) * CHUNK)
                if s:
                    pe.wait_ge(v_new_ready, s)
                else:
                    pe.wait_ge(solutions_copied, 2)
                    pe.wait_ge(qg_ready, 1)
                vn = v_new[b] if s else u_sol
                if s < LAST_STEP:
                    for h in range(HEADS):
                        i = mm(ACC[1][:, h * P:(h + 1) * P], one(k_g, b, h)[rows, :], vn[rows, h * P:(h + 1) * P],
                               start=True, stop=True)
                    i.then_inc(state_added, 1)
                for h in range(HEADS):
                    dst = ACC[2 + b][:, h * P + j * CHUNK:h * P + (j + 1) * CHUNK]
                    if s:
                        mm(dst, state[s % 2][:, h * P:(h + 1) * P], one(qg_t, b, h)[:, rows], start=True,
                           stop=False)
                    i = mm(dst, vn[rows, h * P:(h + 1) * P], one(attn, b, h)[rows, rows], start=(s == 0), stop=True)
                if j == JC - 1:
                    i.then_inc(o_ready, 1)
            if name[:5] == "o_sum":
                b = int(name[5:])
                pe.wait_ge(o_squared, b + 1)
                for h in range(HEADS):
                    i = mm(AUX2[:, h:h + 1], sq[:, 2 + b, h * P:(h + 1) * P], ones[:, 0:1], start=True, stop=True)
                i.then_inc(o_summed, 1)
            if name[:5] == "o_row":
                b = int(name[5:])
                pe.wait_ge(o_diagonal, b + 1)
                mm(AUX2[:], ones[:], o_diag[:, b * 512:(b + 1) * 512], start=True, stop=True) \
                  .then_inc(o_rows_ready, 1)
            if name == "solutions":
                pe.wait_ge(inverse_t_ready, N_LEVEL)
                pe.wait_ge(v_scaled, 1)
                for k, (banks, what) in enumerate(((ACC[0:2], v_b), (ACC[2:4], kb_g))):
                    for b in range(TB):
                        for h in range(HEADS):
                            st, mv = one(inv_t, b, h), one(what, b, h)
                            if k:
                                st, mv = mv, st
                            i = mm(banks[b][:, h * P:(h + 1) * P], st, mv, start=True, stop=True)
                    i.then_inc(solved, 1)

        def hyb_vector_phase(dve, name):
            v = nc.vector

            if name == "gates":
                dve.wait_ge(gates_projected, 1)
                v.tensor_tensor(ba_row[:], AUX2[:, 0:SEQ], rstd[:, 0:SEQ], ALU.mult).then_inc(gates_scaled, 1)
            if name == "gates_turned":
                dve.wait_ge(gates_turned, 1)
                turned = AUX2[:, 0:2 * P].rearrange("p (b c) -> p b c", b=TB)
                v.tensor_copy(tiny[:, T_B, :].rearrange("p (b h) -> p b h", b=TB), turned[:, :, 0:HEADS])
                v.tensor_copy(tiny[:, T_A, :].rearrange("p (b h) -> p b h", b=TB),
                              turned[:, :, HEADS:2 * HEADS]).then_inc(vector_step, 1)
                dve.wait_ge(vector_step, next(steps))
                for b in range(TB):
                    o = b * HEADS
                    i = v.tensor_tensor(tiny[:, T_Y, o:o + HEADS], tiny[:, T_A, o:o + HEADS], gate_par[:, 1, :],
                                        ALU.add)
                i.then_inc(vector_step, 1)
                dve.wait_ge(vector_step, next(steps))
                v.scalar_tensor_tensor(out=ty(T_NEG), in0=ty(T_Y), scalar=-1.0, in1=ty(T_Y), op0=ALU.mult,
                                       op1=ALU.min).then_inc(minus_abs, 1)
            if name == "gates_logged":
                dve.wait_ge(log_ready, 1)
                v.tensor_scalar(ty(T_W), ty(T_U), 1.0, None, ALU.add).then_inc(vector_step, 1)
                dve.wait_ge(vector_step, next(steps))
                v.scalar_tensor_tensor(out=ty(T_D), in0=ty(T_W), scalar=-1.0, in1=ty(T_U), op0=ALU.add,
                                       op1=ALU.subtract).then_inc(vector_step, 1)
                dve.wait_ge(vector_step, next(steps))
                v.reciprocal(ty(T_R), ty(T_W)).then_inc(vector_step, 1)
                dve.wait_ge(vector_step, next(steps))
                v.tensor_tensor(ty(T_D), ty(T_D), ty(T_R), ALU.mult).then_inc(vector_step, 1)
                dve.wait_ge(vector_step, next(steps))
                v.tensor_tensor(ty(T_X), ty(T_LN), ty(T_D), ALU.subtract).then_inc(vector_step, 1)
                dve.wait_ge(vector_step, next(steps))
                v.scalar_tensor_tensor(out=ty(T_X), in0=ty(T_Y), scalar=0.0, in1=ty(T_X), op0=ALU.max,
                                       op1=ALU.add).then_inc(vector_step, 1)
                dve.wait_ge(vector_step, next(steps))
                for b in range(TB):
                    o = b * HEADS
                    i = v.scalar_tensor_tensor(out=tiny[:, T_G, o:o + HEADS], in0=tiny[:, T_X, o:o + HEADS],
                                               scalar=-1.0, in1=gate_par[:, 2, :], op0=ALU.mult, op1=ALU.mult)
                i.then_inc(g_ready, 1)
                dve.wait_ge(g_ready, 1)
                v.tensor_tensor(cube(g_diag), table(K_TRI, NS), wide(ty(T_G)), ALU.mult) \
                  .then_inc(diagonals_ready, 1)
                v.tensor_scalar(ty(T_EB), ty(T_EB), 1.0, None, ALU.add).then_inc(vector_step, 1)
                dve.wait_ge(vector_step, next(steps))
                v.reciprocal(ty(T_BETA), ty(T_EB)).then_inc(vector_step, 1)
                dve.wait_ge(vector_step, next(steps))
            if name == "scalars":
                dve.wait_ge(g_summed, 1)
                v.tensor_copy(ty(T_GC), AUX2[:, 16:24])
                v.tensor_copy(ty(T_GL), AUX2[:, 24:32]).then_inc(g_copied, 1)
                dve.wait_ge(g_copied, 1)
                dve.wait_ge(kq_squared, 1)
                v.tensor_reduce(tiny[:, T_RK:T_RQ + 1, :].rearrange("p k n -> p (k n)"),
                                sq[:].rearrange("p b (h s) -> p (b h) s", s=P), AX.X, ALU.add) \
                                  .then_inc(vector_step, 1)
                dve.wait_ge(vector_step, next(steps))
                v.tensor_scalar(ty(T_RK), ty(T_RK), 1e-6, None, ALU.add)
                v.tensor_scalar(ty(T_RQ), ty(T_RQ), 1e-6, float(DK), ALU.add, ALU.mult).then_inc(vector_step, 1)
                dve.wait_ge(vector_step, next(steps))
                v.reciprocal(tiny[:, T_RK:T_RQ + 1, :], tiny[:, T_RK:T_RQ + 1, :])
                v.tensor_tensor(ty(T_GL), ty(T_GL), ty(T_GC), ALU.subtract).then_inc(norms_inverted, 1)
                dve.wait_ge(rows_summed, 1)
                for b in range(TB):
                    i = v.tensor_tensor(by_pair(decay, b), bank_pair((AUX, AUX2)[b]), spread(ty(T_GC), b),
                                        ALU.subtract)
                i.then_inc(vector_step, 1)
                dve.wait_ge(vector_step, next(steps))
                v.tensor_scalar(decay, decay, 0.0, None, ALU.min).then_inc(decay_arg, 1)
                dve.wait_ge(norms_rooted, 1)
                v.tensor_tensor(ty(T_R1), ty(T_RK), ty(T_BETA), ALU.mult).then_inc(vector_step, 1)
                dve.wait_ge(vector_step, next(steps))
                for which, dst, factor in ((1, qs_tok, T_RQ), (0, kb_tok, T_R1)):
                    for b in range(TB):
                        i = v.tensor_tensor(by_pair(dst, b), bank_pair(ACC[2 * which + b]), spread(ty(factor), b),
                                            ALU.mult)
                    i.then_inc(kq_scaled, 1)
            if name == "rows":
                dve.wait_ge(rows_exp, 1)
                v.tensor_tensor(cube(decay), cube(decay), wide(ty(T_RK)), ALU.mult).then_inc(vector_step, 1)
                dve.wait_ge(vector_step, next(steps))
                v.tensor_tensor(cube(decay), cube(decay), table(K_TRI, NS), ALU.mult).then_inc(decay_ready, 1)
                dve.wait_ge(gates_raised, 1)
                v.tensor_tensor(ty(T_F2), ty(T_RK), ty(T_EKG), ALU.mult)
                v.scalar_tensor_tensor(out=ty(T_F1), in0=ty(T_R1), scalar=-1.0, in1=ty(T_EGC), op0=ALU.mult,
                                       op1=ALU.mult).then_inc(vector_step, 1)
                dve.wait_ge(vector_step, next(steps))
                for b in range(TB):
                    i = v.tensor_tensor(by_pair(k_g, b), bank_pair(ACC[b]), spread(ty(T_F2), b), ALU.mult)
                i.then_inc(k_scaled, 1)
                for b in range(TB):
                    i = v.tensor_tensor(by_pair(kb_g, b), bank_pair(ACC[b]), spread(ty(T_F1), b), ALU.mult)
                i.then_inc(k_scaled, 1)
            if name == "products":
                dve.wait_ge(decay_ready, 1)
                dve.wait_ge(pair_products, 1)
                for b in range(TB):
                    i = v.tensor_tensor(by_pair(lower, b), bank_pair((AUX, AUX2)[b]), by_pair(decay, b), ALU.mult)
                i.then_inc(pairs_masked, 1)
                dve.wait_ge(pairs_masked, 1)
                v.tensor_tensor(cube(inv_t), cube(lower), table(K_LEVEL, NS), ALU.mult).then_inc(vector_step, 1)
                dve.wait_ge(vector_step, next(steps))
                v.tensor_tensor(cube(inv_t), table(K_IDENT, NS), cube(inv_t), ALU.subtract) \
                  .then_inc(inverse_t_ready, 1)
                dve.wait_ge(pair_products, 2)
                for b in range(TB):
                    i = v.tensor_tensor(by_pair(attn, b), bank_pair(ACC[2 + b]), by_pair(decay, b), ALU.mult)
                i.then_inc(pairs_masked, 1)
            if name == f"right{N_LEVEL - 1}":
                dve.wait_ge(v_turned, 1)
                for b in range(TB):
                    i = v.tensor_tensor(by_pair(v_b, b), bank_pair(ACC[2 + b]), spread(ty(T_BETA), b), ALU.mult)
                i.then_inc(v_scaled, 1)
            if name[:5] == "right":
                n = int(name[5:])
                for b in range(TB):
                    dve.wait_ge(right_done, TB * (n - 1) + b + 1)
                    if n < N_LEVEL - 1:
                        i = v.tensor_tensor(by_pair(inv, b), by_pair(inv, b), bank_pair(ACC[2 + b]), ALU.subtract)
                if n < N_LEVEL - 1:
                    i.then_inc(inverse_ready, 1)
                for b in range(TB):
                    i = v.tensor_tensor(by_pair(inv_t, b), by_pair(inv_t, b), bank_pair(ACC[b]), ALU.subtract)
                i.then_inc(inverse_t_ready, 1)

            if name[:4] == "read":
                s = int(name[4:])
                b, j = divmod(s, JC)
                rows = slice(j * CHUNK, (j + 1) * CHUNK)
                dve.wait_ge(state_read, s)
                v.tensor_tensor(v_new[b][rows, :], ACC[0][rows, :], u_sol[rows, b * 512:(b + 1) * 512],
                                ALU.add).then_inc(v_new_ready, 1)
            if name[:3] == "add":
                s = int(name[3:])
                b, j = divmod(s, JC)
                last = j * CHUNK + CHUNK - 1
                new, old = state[(s + 1) % 2], state[s % 2]
                dve.wait_ge(rows_exp, 3)
                dve.wait_ge(state_added, s + 1)
                if s == 0:
                    i = v.tensor_copy(new, ACC[1][:])
                else:
                    for h in range(HEADS):
                        cols = slice(h * P, (h + 1) * P)
                        i = v.scalar_tensor_tensor(out=new[:, cols], in0=old[:, cols],
                                                   scalar=one(g_exp, b, h)[:, last:last + 1],
                                                   in1=ACC[1][:, cols], op0=ALU.mult, op1=ALU.add)
                i.then_inc(state_ready, 1)
                dve.wait_ge(state_ready, s + 1)

        def hyb_scalar_phase(act_e, name):
            a = nc.scalar.activation

            if name == "gates_turned":
                a(gate_par[:, 2, :], gate_par[:, 0, :], ACT.Exp)
                act_e.wait_ge(minus_abs, 1)
                a(ty(T_EB), ty(T_B), ACT.Exp, scale=-1.0)
                a(ty(T_U), ty(T_NEG), ACT.Exp).then_inc(gates_exp, 1)
                act_e.wait_ge(gates_exp, 1)
                a(ty(T_LN), ty(T_U), ACT.Ln, bias=1.0).then_inc(log_ready, 1)
            if name == "scalars":
                act_e.wait_ge(kq_turned, 1)
                for k in range(2 * TB):
                    i = a(sq[:, k, :], ACC[k][:], ACT.Square)
                i.then_inc(kq_squared, 1)
                act_e.wait_ge(norms_inverted, 1)
                a(tiny[:, T_RK:T_RQ + 1, :], tiny[:, T_RK:T_RQ + 1, :], ACT.Sqrt).then_inc(norms_rooted, 1)
                a(ty(T_EGC), ty(T_GC), ACT.Exp)
                a(ty(T_EKG), ty(T_GL), ACT.Exp).then_inc(gates_raised, 1)
                act_e.wait_ge(decay_arg, 1)
                a(decay, decay, ACT.Exp).then_inc(rows_exp, 1)
                for b in range(TB):
                    a(by_pair(g_exp, b), bank_pair((AUX, AUX2)[b]), ACT.Exp).then_inc(rows_exp, 1)
            if name == "rows":
                for k, (banks, dst) in enumerate(((ACC[2:4], qs_t), ((AUX, AUX2), kb_t))):
                    act_e.wait_ge(kq_turned_back, k + 1)
                    for b in range(TB):
                        i = a(by_pair(dst, b), bank_pair(banks[b]), ACT.Copy)
                    i.then_inc(kq_copied, 1)
            if name == "start":
                act_e.wait_ge(inverse_turned, 1)
                for b in range(TB):
                    i = a(by_pair(inv, b), bank_pair((AUX, AUX2)[b]), ACT.Copy)
                i.then_inc(inverse_ready, 1)
            if name[:4] == "left":
                n = int(name[4:])
                for b in range(TB):
                    act_e.wait_ge(left_done, TB * (n - 1) + b + 1)
                    a(by_pair(prod, b), bank_pair((AUX, AUX2)[b]), ACT.Copy).then_inc(left_copied, 1)
            if name == "solutions":
                for k, (banks, dst) in enumerate(((ACC[0:2], u_sol), (ACC[2:4], w_sol))):
                    act_e.wait_ge(solved, k + 1)
                    for b in range(TB):
                        i = a(by_pair(dst, b), bank_pair(banks[b]), ACT.Copy)
                    i.then_inc(solutions_copied, 1)

        def hyb_pool_phase(pool, name):
            if name == "rows":
                pool.wait_ge(kq_copied, 2)
                pool.wait_ge(rows_exp, 3)
                nc.gpsimd.tensor_tensor(qg_t, qs_t, g_exp, ALU.mult).then_inc(qg_ready, 1)
            if name == "products":
                pool.wait_ge(pairs_masked, 2)
            if name == "start" or name[:4] == "left":
                n = 1 if name == "start" else int(name[4:]) + 1
                if n < N_LEVEL:
                    if n > 2:
                        pool.wait_ge(left_done, TB * (n - 2))
                    if n == 1:
                        pool.wait_ge(kq_copied, 2)
                    nc.gpsimd.tensor_tensor(cube(step_m[n % 2]), cube(lower), table(K_LEVEL + P * n, NS),
                                            ALU.mult).then_inc(level_masked, 1)

        def hyb_tensor(pe, n):
            c = first["hyb_in"]
            pe.wait_ge(rest_loaded, 16 * 5)
            for m in range(HYB_IN):
                if m >= 2:
                    pe.wait_ge(hyb_evacuated, m - 1)
                halfway = HYB_PLAN.get((m, 0), [])
                column_chunk(pe, (c + m, 0), (GATE, UP)[m % 2], h_hi, h_lo,
                             (h_ready, PAIRS * n) if m == 0 else None,
                             (lambda: [hyb_tensor_phase(pe, x) for x in halfway]) if halfway else None)
                if m == 0:
                    norm_ss(pe, n)
                for x in HYB_PLAN.get((m, 1), []):
                    hyb_tensor_phase(pe, x)

            mm = nc.tensor.matmul

            def out_part(j, tiles, fts, opens, toks=slice(0, SEQ), part=None):
                ch = (first["hyb_out"] + j, 0)
                pe.wait_ge(hi_split if part == 0 else lo_split, number(ch) + 1)
                for ft in fts:
                    for kt in tiles:
                        i = product(OUT_BANKS[j][:, ft * SEQ + toks.start:ft * SEQ + toks.stop], slot(ch),
                                    slice(kt * CW + ft * P, kt * CW + (ft + 1) * P), m_hi[:, kt, toks],
                                    m_lo[:, kt, toks], start=(opens and ft == 0 and kt == tiles[0]), part=part)
                return i

            pe.wait_ge(hyb_evacuated, HYB_IN)
            pe.wait_ge(conv_split, 1)
            conv_tiles, head_tiles = [4, 5, 6, 7], [0, 1, 2, 3]
            out_part(0, conv_tiles, [0], True)
            hyb_tensor_phase(pe, "add1")
            out_part(0, conv_tiles, [1], False)
            hyb_tensor_phase(pe, "read2")
            hyb_tensor_phase(pe, "o_sum0")
            out_part(1, conv_tiles, [0], True)
            hyb_tensor_phase(pe, "add2")
            hyb_tensor_phase(pe, "o_row0")
            out_part(1, conv_tiles, [1], False)
            hyb_tensor_phase(pe, "read3")
            out_part(2, conv_tiles, [0], True)
            hyb_tensor_phase(pe, "add3")
            out_part(2, conv_tiles, [1], False)
            hyb_tensor_phase(pe, "o_sum1")
            toks = [slice(b * P, (b + 1) * P) for b in range(TB)]
            pe.wait_ge(o_split, 1)
            out_part(0, head_tiles, range(HG), False, toks[0])
            hyb_tensor_phase(pe, "o_row1")
            out_part(1, head_tiles, range(HG), False, toks[0])
            out_part(2, head_tiles, range(HG), False, toks[0])
            pe.wait_ge(o_split, TB)
            for j in range(RING):
                out_part(j, head_tiles, range(HG), False, toks[1]).then_inc(w_used, 1)
            out_part(RING, conv_tiles + head_tiles, range(HG), True, part=0)
            out_part(RING, conv_tiles + head_tiles, range(HG), False, part=1).then_inc(w_used, 1)

        def hyb_scalar(act_e, n):
            c = first["hyb_in"]

            def silu_conv(kind, half):
                act_e.wait_ge(conv_done[kind], half + 1)
                tile = conv_out[kind][:, half * 512:(half + 1) * 512]
                nc.scalar.activation(tile, tile, ACT.Silu).then_inc(v_silu if kind == "v" else kq_silu, 1)

            for m in range(HYB_IN):
                for x in HYB_PLAN.get((m, 0), []):
                    hyb_scalar_phase(act_e, x)
                if KINDS[(m - 1) // 2] == "v" and m:
                    silu_conv("v", (m - 1) % 2)
                split_hi(act_e, (c + m + RING, 0))
                kind = KINDS[m // 2]
                if m >= 4:
                    for x in HYB_PLAN.get((m, 1), []):
                        hyb_scalar_phase(act_e, x)
                if kind in "kq":
                    silu_conv(kind, m % 2)
                if m >= 12:
                    act_e.wait_ge(hyb_evacuated, m + 1)
                    o = (m - 12) * 512
                    nc.scalar.activation(z_t[:, o:o + 512], z_t[:, o:o + 512], ACT.Silu).then_inc(z_silu, 1)
                if m == 12:
                    act_e.wait_ge(conv_gated, 2)
                    nc.scalar.activation(m_hi[:, 4:8, :].rearrange("p a b -> p (a b)"), y_sc, ACT.Copy) \
                      .then_inc(conv_hi_ready, 1)
                if m < 4:
                    for x in HYB_PLAN.get((m, 1), []):
                        hyb_scalar_phase(act_e, x)
            for b in range(TB):
                act_e.wait_ge(o_ready, b + 1)
                nc.scalar.activation(sq[:, 2 + b, :], ACC[2 + b][:], ACT.Square).then_inc(o_squared, 1)
                act_e.wait_ge(o_inverted, b + 1)
                o = b * HEADS
                nc.scalar.activation(tiny[:, T_RO, o:o + HEADS], tiny[:, T_OS, o:o + HEADS], ACT.Sqrt) \
                  .then_inc(o_rooted, 1)
                act_e.wait_ge(o_final, b + 1)
                nc.scalar.activation(m_hi[:, 0:4, b * P:(b + 1) * P], by_tile(o_gated)[:, :, b * P:(b + 1) * P],
                                     ACT.Copy).then_inc(o_hi_ready, 1)

        def hyb_vector(dve, n):
            v = nc.vector
            c = first["hyb_in"]

            dve.wait_ge(rest_loaded, 16 * 5)

            def evacuate(m, dst):
                dve.wait_ge(w_used, c + m + 1)
                i = v.tensor_tensor(dst.rearrange("p (a s) -> p a s", a=2),
                                    (GATE, UP)[m % 2][:].rearrange("p (a s) -> p a s", a=2),
                                    over_rows(rstd[:, 0:SEQ], 2), ALU.mult)
                i.then_inc(hyb_evacuated, 1)

            def conv(src, dst, taps, weight, tiles, done):
                for s in range(taps):
                    for x in tiles:
                        a, d = src[:, x * SEQ:(x + 1) * SEQ], dst[:, x * SEQ:(x + 1) * SEQ]
                        if s == 0:
                            i = v.tensor_scalar(d, a, weight(s, x), None, ALU.mult)
                        else:
                            i = v.scalar_tensor_tensor(out=d[:, s:], in0=a[:, 0:SEQ - s], scalar=weight(s, x),
                                                       in1=d[:, s:], op0=ALU.mult, op1=ALU.add)
                    if s < taps - 1:
                        i.then_inc(vector_step, 1)
                        dve.wait_ge(vector_step, next(steps))
                    else:
                        i.then_inc(done, 1)

            for m in range(HYB_IN):
                for x in HYB_PLAN.get((m, 0), []):
                    hyb_vector_phase(dve, x)
                o = (m % 2) * 512
                span = slice(o, o + 512)
                tiles = (2 * (m % 2), 2 * (m % 2) + 1)
                kind = KINDS[m // 2]
                evacuate(m, {"c": sc_c, "z": z_t}[kind][:, span] if kind in "cz" else
                         conv_in[kind][:, span] if kind in conv_in else sc_tmp[m % 2][:])
                if m == 0 or m >= 4:
                    for x in HYB_PLAN.get((m, 1), []):
                        hyb_vector_phase(dve, x)
                if kind in conv_in:
                    dve.wait_ge(hyb_evacuated, m + 1)
                    base = V_CONV + {"k": 4, "q": 0, "v": 8}[kind]
                    conv(conv_in[kind], conv_out[kind], 4,
                         lambda s, x: vecT[:, base + 12 * (3 - s) + x:base + 12 * (3 - s) + x + 1],
                         tiles, conv_done[kind])
                if kind == "h":
                    dve.wait_ge(hyb_evacuated, m + 1)
                    v.tensor_tensor(sc_u[:, span], sc_tmp[m % 2][:], sc_c[:, span], ALU.mult) \
                      .then_inc(vector_step, 1)
                    dve.wait_ge(vector_step, next(steps))
                    conv(sc_u, sc_conv, 3, lambda s, x: vecT[:, V_SC + 4 * (2 - s) + x:V_SC + 4 * (2 - s) + x + 1],
                         tiles, sc_conv_done)
                if kind == "b":
                    dve.wait_ge(hyb_evacuated, m + 1)
                    dve.wait_ge(sc_conv_done, m % 2 + 1)
                    v.tensor_tensor(y_sc[:, span], sc_tmp[m % 2][:], sc_conv[:, span], ALU.mult) \
                      .then_inc(conv_gated, 1)
                if m == 12:
                    dve.wait_ge(conv_hi_ready, 1)
                    v.tensor_tensor(m_lo[:, 4:8, :].rearrange("p a b -> p (a b)"), y_sc,
                                    m_hi[:, 4:8, :].rearrange("p a b -> p (a b)").bitcast(F32),
                                    ALU.subtract).then_inc(conv_split, 1)
                if 0 < m < 4:
                    for x in HYB_PLAN.get((m, 1), []):
                        hyb_vector_phase(dve, x)

            def o_scale(b):
                o = b * HEADS
                dve.wait_ge(o_summed, b + 1)
                v.tensor_scalar(tiny[:, T_OS, o:o + HEADS], AUX2[:, 0:HEADS], 1.0 / DK, EPS, ALU.mult, ALU.add) \
                  .then_inc(vector_step, 1)
                dve.wait_ge(vector_step, next(steps))
                v.reciprocal(tiny[:, T_OS, o:o + HEADS], tiny[:, T_OS, o:o + HEADS]).then_inc(o_inverted, 1)

            def o_spread(b):
                dve.wait_ge(o_rooted, b + 1)
                v.tensor_tensor(by_pair(o_diag, b), table(K_IDENT, HEADS), spread(ty(T_RO), b), ALU.mult) \
                  .then_inc(o_diagonal, 1)

            def o_gate(b):
                dve.wait_ge(z_weighted, 1)
                dve.wait_ge(o_squared, b + 1)
                v.tensor_tensor(by_tile(o_gated)[:, :, b * P:(b + 1) * P], bank_pair(ACC[2 + b]),
                                by_tile(z_t)[:, :, b * P:(b + 1) * P], ALU.mult).then_inc(o_gate_done, 1)

            def o_finish(b):
                dve.wait_ge(o_rows_ready, b + 1)
                dve.wait_ge(o_gate_done, b + 1)
                part = by_tile(o_gated)[:, :, b * P:(b + 1) * P]
                v.tensor_tensor(part, part, bank_pair(AUX2), ALU.mult).then_inc(o_final, 1)

            def o_rest(b):
                dve.wait_ge(o_final, b + 1)
                dve.wait_ge(o_hi_ready, b + 1)
                v.tensor_tensor(m_lo[:, 0:4, b * P:(b + 1) * P], by_tile(o_gated)[:, :, b * P:(b + 1) * P],
                                m_hi[:, 0:4, b * P:(b + 1) * P].bitcast(F32), ALU.subtract).then_inc(o_split, 1)

            hyb_vector_phase(dve, "add1")
            hyb_vector_phase(dve, "read2")
            o_scale(0)
            o_spread(0)
            o_gate(0)
            hyb_vector_phase(dve, "add2")
            o_finish(0)
            hyb_vector_phase(dve, "read3")
            o_rest(0)
            o_gate(1)
            o_scale(1)
            o_spread(1)
            o_finish(1)
            o_rest(1)

        def hyb_pool(pool):
            for m in range(HYB_IN):
                for x in HYB_PLAN.get((m, 0), []):
                    hyb_pool_phase(pool, x)
                split_lo(pool, (first["hyb_in"] + m + RING, 0), nc.gpsimd, handed_over=(m == 0))
                for x in HYB_PLAN.get((m, 1), []):
                    hyb_pool_phase(pool, x)
            pool.wait_ge(z_silu, 2)
            pool.wait_ge(vec_ready, 2)
            nc.gpsimd.tensor_scalar(z_t, z_t, vecT[:, V_GN:V_GN + 1], None, ALU.mult).then_inc(z_weighted, 1)

        HD = 64
        KV = t["swa_w_qkv"].shape[2] // HD // 6
        GRP = 4
        QW = KV * GRP * HD
        SWA_COLS = [QW, QW + CW] + [g * CW for g in range(KV)]
        SCALE = float(HD) ** -0.5
        b_qkv = work[:, 0:QW + 2 * CW]
        k_pad = work[:, 1536:3072].rearrange("p (b g d) -> p b g d", b=TB, g=KV)
        v_tok = work[:, 3072:3584].rearrange("p (b c) -> p b c", b=TB)
        q_tok = [work[:, 3584 + 512 * n:4096 + 512 * n] for n in range(2)]
        qT = [work[:, 4608 + 512 * n:5120 + 512 * n] for n in range(2)]
        kT = [work[:, 5632 + 1024 * n:6656 + 1024 * n] for n in range(2)]
        score = [work[:, 7680 + 1536 * n:9216 + 1536 * n] for n in range(2)]
        prob_t = [work[:, 10752:12288], work[:, 13504:15040]]
        o_tok = [work[:, 12288 + 512 * n:12800 + 512 * n] for n in range(2)]
        sinks = sb("swa_sink_cols", [P, KV * GRP])
        att = work[:, 13312:13312 + 48 * KV].rearrange("p (k n h) -> p k n h", k=6, h=GRP)
        A_MAX, A_NEG, A_SUM, A_SINK, A_DEN, A_INV = range(6)

        def stat(k, g, b=None):
            if b is None:
                return att[:, k, 2 * g:2 * g + 2, :]
            return att[:, k, 2 * g + b, :]

        def score_part(g, b):
            s = score[g % 2]
            return (s[:, 0:512] if b == 0 else s[:, 512:1536]).rearrange("p (h k) -> p h k", h=GRP)

        def head_tok(ap):
            return ap.rearrange("p (b h d) -> p b h d", b=TB, d=HD)

        def angles(col, lo, hi):
            a = kon[:, col:col + 128].rearrange("p (b h d) -> p b h d", b=TB, h=1)[:, :, :, lo:hi]
            return a.to_broadcast([P, TB, GRP, hi - lo])

        def swa_sync(sp):
            w = t["swa_w_qkv"][0].rearrange("(k p) f -> p k f", p=P)
            for m in range(SWA_IN):
                if m == 1:
                    sp.wait_ge(w_used, first["ffn2"] + 1)
                    sp.dma_start(b_qkv, t["swa_b_qkv"][0].partition_broadcast(P)).then_inc(bias_loaded, 16)
                load(sp, (first["swa_in"] + m, 0), w[:, :, SWA_COLS[m]:SWA_COLS[m] + CW])
            w = t["swa_w_o"][0].rearrange("(k p) f -> p k f", p=P)
            for m in range(SWA_OUT):
                load(sp, (first["swa_out"] + m, 0), w[:, :, m * CW:(m + 1) * CW])

        def swa_tensor(pe, n):
            c = first["swa_in"]
            mm, turn = nc.tensor.matmul, nc.tensor.transpose

            def token_chunk(m, half=None):
                if m >= 2:
                    pe.wait_ge(swa_evacuated, m - 1)
                ch = (c + m, 0)
                bk, s = (GATE, UP)[m % 2], slot(ch)

                def step(kt, b, passes, start=False, stop=False):
                    for n_pass in passes:
                        st, mv = ((h_hi, w_hi), (h_lo, w_hi), (h_hi, w_lo))[n_pass]
                        i = mm(bk[:, b * CW:(b + 1) * CW], st[:, kt, b * P:(b + 1) * P],
                               mv[s][:, kt * CW:(kt + 1) * CW], start=(start and n_pass == 0),
                               stop=(stop and n_pass == 2), skip_group_check=True)
                    return i

                if m == 0:
                    pe.wait_ge(hi_split, number(ch) + 1)
                    for kt in range(KT):
                        if kt % 2 == 0:
                            pe.wait_ge(h_ready, PAIRS * n + kt // 2 + 1)
                        for b in range(TB):
                            step(kt, b, (0, 1), start=(kt + b == 0))
                pe.wait_ge(lo_split, number(ch) + 1)
                for b in range(TB):
                    if half is not None and b == 1:
                        half()
                    for kt in range(KT):
                        i = step(kt, b, (2,) if m == 0 else (0, 1, 2), start=(m > 0 and kt + b == 0),
                                 stop=(kt == KT - 1))
                i.then_inc(w_used, 1)

            def turn_k():
                pe.wait_ge(k_rotated, 1)
                pe.wait_ge(k_padded, 1)
                for par in range(2):
                    for b in range(TB):
                        if par:
                            pe.wait_ge(k_copied, b + 1)
                        for g in range(KV):
                            o = 64 * (1 - par)
                            i = turn((AUX, AUX2)[b][:, g * P:(g + 1) * P], k_pad[:, b, g, o:o + P], ident)
                        i.then_inc(k_transposed, 1)

            def turn_q(g):
                pe.wait_ge(q_rotated, g + 1)
                if g:
                    pe.wait_ge(q_copied, g)
                else:
                    pe.wait_ge(k_copied, 3)
                for x in range(2):
                    for b in range(TB):
                        i = turn(AUX[:, x * SEQ + b * P:x * SEQ + (b + 1) * P],
                                 q_tok[g % 2][:, b * CW + x * P:b * CW + (x + 1) * P], ident)
                i.then_inc(q_transposed, 1)

            def scores(g):
                if g == 0:
                    pe.wait_ge(k_copied, 4)
                elif g == 1:
                    pe.wait_ge(scores_read, 1)
                else:
                    pe.wait_ge(prob_copied, 2 * (g - 1))
                pe.wait_ge(q_copied, g + 1)
                for h in range(GRP):
                    q = qT[g % 2][:, (h // 2) * SEQ:(h // 2 + 1) * SEQ]
                    k = kT[h % 2][:, g * SEQ:(g + 1) * SEQ]
                    mm(ACC[h // 2][:, (h % 2) * SEQ:(h % 2 + 1) * SEQ], q[:, P:2 * P], k, start=True, stop=True)
                for h in range(GRP):
                    q = qT[g % 2][:, (h // 2) * SEQ:(h // 2 + 1) * SEQ]
                    k = kT[h % 2][:, g * SEQ:(g + 1) * SEQ]
                    i = mm(ACC[2][:, h * P:(h + 1) * P], q[:, 0:P], k[:, 0:P], start=True, stop=True)
                i.then_inc(scores_ready, 1)

            def turn_probs(g):
                pe.wait_ge(probs_ready, g + 1)
                if g < KV - 1:
                    pe.wait_ge(scores_read, g + 2)
                else:
                    pe.wait_ge(prob_copied, 2 * g)
                for kb in range(2):
                    for h in range(GRP):
                        i = turn(ACC[kb][:, h * P:(h + 1) * P], score_part(g, 1)[:, h, kb * P:(kb + 1) * P], ident)
                for h in range(GRP):
                    i = turn(ACC[2][:, h * P:(h + 1) * P], score_part(g, 0)[:, h, :], ident)
                i.then_inc(probs_transposed, 1)

            def values(g):
                pe.wait_ge(prob_copied, 2 * g + 2)
                if g:
                    pe.wait_ge(o_normed, g)
                for h in range(GRP):
                    def p_t(k):
                        return prob_t[g % 2][:, k * 512 + h * P:k * 512 + (h + 1) * P]
                    v = v_tok[:, :, g * HD:(g + 1) * HD]
                    mm(ACC[3][:, CW + h * HD:CW + (h + 1) * HD], p_t(0), v[:, 0, :], start=True, stop=False)
                    mm(ACC[3][:, CW + h * HD:CW + (h + 1) * HD], p_t(1), v[:, 1, :], start=False, stop=True)
                    i = mm(ACC[3][:, h * HD:(h + 1) * HD], p_t(2), v[:, 0, :], start=True, stop=True)
                i.then_inc(values_summed, 1)

            def turn_o(g):
                pe.wait_ge(o_normed, g + 1)
                if g:
                    pe.wait_ge(o_lo_done, g)
                for x in range(2):
                    for b in range(TB):
                        i = turn(AUX2[:, x * SEQ + b * P:x * SEQ + (b + 1) * P],
                                 o_tok[g % 2][:, b * CW + x * P:b * CW + (x + 1) * P], ident)
                i.then_inc(o_transposed, 1)

            def out_part(j, g, tiles, part=None):
                ch = (first["swa_out"] + j, 0)
                pe.wait_ge(hi_split if part == 0 else lo_split, number(ch) + 1)
                pe.wait_ge(o_lo_done, g + 1)
                for ft in range(HG):
                    for kt in tiles:
                        i = product(OUT_BANKS[j][:, ft * SEQ:(ft + 1) * SEQ], slot(ch),
                                    slice(kt * CW + ft * P, kt * CW + (ft + 1) * P), m_hi[:, kt, :], m_lo[:, kt, :],
                                    start=(ft == 0 and kt == 0), part=part)
                return i

            def out(g, j):
                if j == 2 and g == 0:
                    pe.wait_ge(q_copied, KV)
                i = out_part(j, g, [2 * g, 2 * g + 1])
                if g == KV - 1:
                    i.then_inc(w_used, 1)

            token_chunk(0)
            norm_ss(pe, n, columns=True)
            token_chunk(1)
            token_chunk(2, turn_k)
            token_chunk(3, lambda: turn_q(0))
            scores(0)
            token_chunk(4, lambda: turn_q(1))
            scores(1)
            token_chunk(5, lambda: (turn_q(2), turn_probs(0)))
            scores(2)
            values(0)
            turn_q(3)
            turn_probs(1)
            turn_o(0)
            scores(3)
            pe.wait_ge(swa_evacuated, SWA_IN)
            out(0, 0)
            out(0, 1)
            values(1)
            turn_probs(2)
            out(0, 2)
            turn_o(1)
            values(2)
            out(1, 0)
            turn_probs(3)
            out(1, 1)
            turn_o(2)
            out(1, 2)
            values(3)
            out(2, 0)
            turn_o(3)
            out(2, 1)
            out(2, 2)
            for j in range(RING):
                out(3, j)
            out_part(RING, KV - 1, range(KT), part=0)
            out_part(RING, KV - 1, range(KT), part=1).then_inc(w_used, 1)

        def swa_scalar(act_e, n):
            a = nc.scalar.activation
            c = first["swa_in"]

            def copy_k():
                for par in range(2):
                    for b in range(TB):
                        act_e.wait_ge(k_transposed, 2 * par + b + 1)
                        dst = kT[par].rearrange("p (g s) -> p g s", g=KV)[:, :, b * P:(b + 1) * P]
                        a(dst, (AUX, AUX2)[b][:].rearrange("p (g s) -> p g s", g=KV), ACT.Copy) \
                          .then_inc(k_copied, 1)

            def copy_q(g):
                act_e.wait_ge(q_transposed, g + 1)
                if g >= 2:
                    act_e.wait_ge(scores_ready, g - 1)
                a(qT[g % 2], AUX[:], ACT.Copy).then_inc(q_copied, 1)

            def exps(g):
                act_e.wait_ge(max_ready, g + 1)
                a(stat(A_DEN, g), stat(A_SINK, g), ACT.Exp)
                for b in range(TB):
                    for h in range(GRP):
                        s = score_part(g, b)[:, h, :]
                        i = a(s, s, ACT.Exp, bias=stat(A_NEG, g, b)[:, h:h + 1], scale=SCALE,
                              accum_out=stat(A_SUM, g, b)[:, h:h + 1])
                i.then_inc(probs_ready, 1)

            def copy_probs(g):
                act_e.wait_ge(probs_transposed, g + 1)
                if g >= 2:
                    act_e.wait_ge(values_summed, g - 1)
                for k in range(2):
                    i = a(prob_t[g % 2][:, k * 512:(k + 1) * 512], ACC[k][:], ACT.Copy)
                i.then_inc(prob_copied, 1)

            def hi_o(g):
                act_e.wait_ge(o_transposed, g + 1)
                a(m_hi[:, 2 * g:2 * g + 2, :].rearrange("p a b -> p (a b)"), AUX2[:], ACT.Copy) \
                  .then_inc(o_hi_done, 1)

            for m in range(SWA_IN):
                if m == 2:
                    copy_k()
                if m >= 3:
                    copy_q(m - 3)
                if m == 4:
                    exps(0)
                if m == 5:
                    copy_probs(0)
                    exps(1)
                split_hi(act_e, (c + m + RING, 0))
            copy_q(3)
            copy_probs(1)
            hi_o(0)
            exps(2)
            copy_probs(2)
            hi_o(1)
            exps(3)
            copy_probs(3)
            hi_o(2)
            hi_o(3)

        def swa_vector(dve, n):
            v = nc.vector
            c = first["swa_in"]

            def evacuate(m, dst):
                dve.wait_ge(w_used, c + m + 1)
                if m == 0:
                    dve.wait_ge(bias_loaded, 16)
                for b in range(TB):
                    i = v.scalar_tensor_tensor(out=dst[:, b * CW:(b + 1) * CW],
                                               in0=(GATE, UP)[m % 2][:, b * CW:(b + 1) * CW],
                                               scalar=rstd[:, SEQ + b:SEQ + b + 1],
                                               in1=b_qkv[:, SWA_COLS[m]:SWA_COLS[m] + CW], op0=ALU.mult, op1=ALU.add)
                i.then_inc(swa_evacuated, 1)

            def rotate(m, dst, done):
                dve.wait_ge(swa_evacuated, m + 1)
                x, s = head_tok(gate[:]), head_tok(silu_r[:])
                h = HD // 2
                v.tensor_tensor(s[:, :, :, 0:h], x[:, :, :, h:HD], angles(K_SIN, 0, h), ALU.mult)
                v.tensor_tensor(s[:, :, :, h:HD], x[:, :, :, 0:h], angles(K_SIN, h, HD), ALU.mult) \
                  .then_inc(vector_step, 1)
                dve.wait_ge(vector_step, next(steps))
                dve.wait_ge(x_cos_ready, 1 if m == 0 else m)
                for b in range(TB):
                    i = v.tensor_tensor(dst(b), head_tok(silu[:])[:, b], s[:, b], ALU.add)
                i.then_inc(done, 1)

            def soft(g):
                dve.wait_ge(scores_ready, g + 1)
                if g >= 2:
                    dve.wait_ge(probs_transposed, g - 1)
                for k in range(2):
                    v.tensor_tensor(score_part(g, 1)[:, 2 * k:2 * k + 2, :],
                                    ACC[k][:].rearrange("p (h k) -> p h k", h=2),
                                    kon[:, K_ATT1:K_ATT1 + 256].rearrange("p (a k) -> p a k", a=1)
                                    .to_broadcast([P, 2, 256]), ALU.add)
                v.tensor_tensor(score_part(g, 0), ACC[2][:].rearrange("p (h k) -> p h k", h=GRP),
                                table(K_ATT0, GRP), ALU.add).then_inc(scores_read, 1)
                dve.wait_ge(scores_read, g + 1)
                for b in range(TB):
                    i = v.tensor_reduce(stat(A_MAX, g, b), score_part(g, b), AX.X, ALU.max)
                i.then_inc(vector_step, 1)
                dve.wait_ge(vector_step, next(steps))
                for b in range(TB):
                    i = v.scalar_tensor_tensor(out=stat(A_MAX, g, b), in0=stat(A_MAX, g, b), scalar=SCALE,
                                               in1=sinks[:, g * GRP:(g + 1) * GRP], op0=ALU.mult, op1=ALU.max)
                i.then_inc(vector_step, 1)
                dve.wait_ge(vector_step, next(steps))
                for b in range(TB):
                    v.tensor_tensor(stat(A_SINK, g, b), sinks[:, g * GRP:(g + 1) * GRP], stat(A_MAX, g, b),
                                    ALU.subtract)
                v.tensor_scalar(stat(A_NEG, g), stat(A_MAX, g), -1.0, None, ALU.mult).then_inc(max_ready, 1)

            def copy_probs(g):
                dve.wait_ge(prob_copied, 2 * g + 1)
                v.tensor_copy(prob_t[g % 2][:, 1024:1536], ACC[2][:]).then_inc(prob_copied, 1)
                v.tensor_tensor(stat(A_DEN, g), stat(A_DEN, g), stat(A_SUM, g), ALU.add) \
                  .then_inc(vector_step, 1)
                dve.wait_ge(vector_step, next(steps))
                v.reciprocal(stat(A_INV, g), stat(A_DEN, g)).then_inc(den_ready, 1)

            def norm_o(g):
                dve.wait_ge(values_summed, g + 1)
                dve.wait_ge(den_ready, g + 1)
                if g >= 2:
                    dve.wait_ge(o_transposed, g - 1)
                for b in range(TB):
                    inv_b = stat(A_INV, g, b).rearrange("p (h d) -> p h d", d=1).to_broadcast([P, GRP, HD])
                    i = v.tensor_tensor(head_tok(o_tok[g % 2])[:, b],
                                        ACC[3][:].rearrange("p (b h d) -> p b h d", b=TB, h=GRP)[:, b], inv_b,
                                        ALU.mult)
                i.then_inc(o_normed, 1)

            def lo_o(g):
                dve.wait_ge(o_hi_done, g + 1)
                v.tensor_tensor(m_lo[:, 2 * g:2 * g + 2, :].rearrange("p a b -> p (a b)"), AUX2[:],
                                m_hi[:, 2 * g:2 * g + 2, :].rearrange("p a b -> p (a b)").bitcast(F32),
                                ALU.subtract).then_inc(o_lo_done, 1)

            dve.wait_ge(k_padded, 1)
            for m in range(SWA_IN):
                if m == 1:
                    evacuate(m, work[:, 3072:3584])
                    split_lo(dve, (c + m + RING, 0), handed_over=True)
                else:
                    if m > 2:
                        dve.wait_ge(x_cos_ready, m - 1)
                    evacuate(m, gate[:])
                if m == 0:
                    rotate(m, lambda b: k_pad[:, b, :, HD:2 * HD], k_rotated)
                if m >= 2:
                    g = m - 2
                    if g >= 2:
                        dve.wait_ge(q_transposed, g - 1)
                    rotate(m, lambda b: head_tok(q_tok[g % 2])[:, b], q_rotated)
                if m == 3:
                    soft(0)
                if m == 4:
                    soft(1)
                    copy_probs(0)
            soft(2)
            norm_o(0)
            copy_probs(1)
            lo_o(0)
            soft(3)
            norm_o(1)
            copy_probs(2)
            lo_o(1)
            norm_o(2)
            copy_probs(3)
            lo_o(2)
            norm_o(3)
            lo_o(3)

        def swa_pool(pool):
            for m in range(SWA_IN):
                if m != 1:
                    pool.wait_ge(swa_evacuated, m + 1)
                    if m:
                        pool.wait_ge(k_rotated, 1) if m == 2 else pool.wait_ge(q_rotated, m - 2)
                    nc.gpsimd.tensor_tensor(head_tok(silu[:]), head_tok(gate[:]), angles(K_COS, 0, HD),
                                            ALU.mult).then_inc(x_cos_ready, 1)
                if m != 1:
                    split_lo(pool, (first["swa_in"] + m + RING, 0), nc.gpsimd, handed_over=True)

        def load_rest(act_e):
            act_e.dma_start(kon[:, P:K_END], t["constants"][:, P:K_END]).then_inc(rest_loaded, 16)
            act_e.dma_start(sinks[:], t["swa_sinks"][0].partition_broadcast(P)).then_inc(rest_loaded, 16)
            act_e.dma_start(gate_par[:, 0, :], t["gdn_a_log"][0].partition_broadcast(P)) \
              .then_inc(rest_loaded, 16)
            act_e.dma_start(gate_par[:, 1, :], t["gdn_dt_bias"][0].partition_broadcast(P)) \
              .then_inc(rest_loaded, 16)
            act_e.wait_ge(wba_cleared, 1)
            act_e.dma_start(wba_pad.rearrange("p (k c) -> p k c", k=KT)[:, :, 0:8],
                            t["hyb_w_in"][0].rearrange("(k p) f -> p k f", p=P)[:, :, 4 * KEY:4 * KEY + 8]) \
                 .then_inc(rest_loaded, 16)

        stages = [("ffn", 0), ("hyb", 0), ("ffn", 1), ("ffn", 2), ("swa", 0), ("ffn", 3)]

        def update(n):
            if n == 0:
                return ACC, [(acc_done, j + 1) for j in range(PAIRS)]
            kind, f = stages[n - 1]
            if kind == "ffn":
                base = PAIRS + (PAIRS - 1) * f
                end = first[f"ffn{f}"] + FFN_CHUNKS
                return ACC, [(acc_done, base + j + 1) for j in range(PAIRS - 1)] + [(w_used, end)]
            c = first[kind + "_out"]
            return OUT_BANKS, [(w_used, c + j + 1) for j in range(PAIRS)]

        block = ctx.enter_context(nc.Block())

        @block.sync
        def _(sp):
            xt = t["x"][0].rearrange("(b p) d -> p b d", p=P)
            sp.dma_start(kon[:, 0:P], t["constants"][:, 0:P]).then_inc(ident_loaded, 16)
            sp.dma_start(x_in[:, :, 0:D // 2], xt[:, :, 0:D // 2]).then_inc(x_loaded, 16)
            sp.dma_start(x_in[:, :, D // 2:D], xt[:, :, D // 2:D]).then_inc(x_loaded2, 16)
            for kind, f in stages:
                (hyb_sync if kind == "hyb" else swa_sync)(sp) if kind != "ffn" else ffn_sync(sp, f)
            sp.wait_ge(w_used, first["ffn3"] + 1)
            sp.dma_start(final_g, t["final_norm"].partition_broadcast(P)).then_inc(final_loaded, 16)
            for b in range(TB):
                for half in range(2):
                    cols = slice(half * 512, (half + 1) * 512)
                    sp.wait_ge(out_ready, 2 * b + half + 1)
                    sp.dma_start(out[b * P:(b + 1) * P, cols], y_out[:, b, cols]).then_inc(stored, 16)
            sp.wait_ge(stored, 16 * 2 * TB)

        @block.gpsimd
        def _(pool):
            nc.gpsimd.memset(ones[:], 1.0).then_inc(set_up, 1)
            nc.gpsimd.memset(neg_half[:], -0.5).then_inc(set_up, 1)
            nc.gpsimd.memset(wba_pad, 0.0).then_inc(wba_cleared, 1)
            pool.wait_ge(set_up, 2)
            for n, (kind, f) in enumerate(stages):
                if kind == "hyb":
                    pool.wait_ge(rest_loaded, 16 * 5)
                    pool.wait_ge(wba_hi_ready, 1)
                    nc.gpsimd.tensor_tensor(wba_lo, wba_pad, wba_hi.bitcast(F32), ALU.subtract) \
                      .then_inc(wba_split, 1)
                if kind == "swa":
                    pool.wait_ge(w_used, first["ffn2"] + 1)
                    nc.gpsimd.memset(work[:, 1536:3072], 0.0).then_inc(k_padded, 1)
                norm_pool(pool, n)
                if kind == "ffn":
                    norm_half(pool, n)
                    ffn_pool(pool, f)
                elif kind == "hyb":
                    hyb_pool(pool)
                else:
                    swa_pool(pool)
            for b in range(TB):
                pool.wait_ge(fin_var, b + 1)
                nc.gpsimd.tensor_tensor(fin_r[:, b:b + 1], fin_v[:, b:b + 1], neg_half[:], ALU.pow) \
                  .then_inc(fin_rstd, 1)


        @block.scalar
        def _(act_e):
            for k, name in enumerate(("ffn1_norm", "mix_norm", "ffn2_norm")):
                rows = vec_rows[k * DEPTH * KT:(k + 1) * DEPTH * KT, :]
                act_e.dma_start(rows, t[name].rearrange("l (k p) -> (l k) p", p=P)) \
                     .then_inc(vec_loaded if k else first_vec_loaded, 16)
            act_e.wait_ge(set_up, 1)
            nc.scalar.activation(fin_ss[:, 0, 0:1], ones[:, 0:1], ACT.Copy)
            act_e.dma_start(vec_rows[V_BO:V_BO + KT, :], t["swa_b_o"][0].rearrange("(k p) -> k p", p=P)) \
                 .then_inc(vec_loaded, 16)
            act_e.dma_start(vec_rows[V_CONV:V_CONV + 48, :],
                            t["gdn_conv_w"][0].rearrange("w (k p) -> (w k) p", p=P)) \
                 .then_inc(vec_loaded, 16)
            act_e.dma_start(vec_rows[V_SC:V_SC + 12, :], t["sc_conv_w"][0].rearrange("w (k p) -> (w k) p", p=P)) \
                 .then_inc(vec_loaded, 16)
            act_e.dma_start(vec_rows[V_GN:V_GN + 1, :], t["gdn_out_norm"]).then_inc(vec_loaded, 16)
            act_e.wait_ge(vec_ready, 1)
            for n, (kind, f) in enumerate(stages):
                c = first[{"ffn": f"ffn{f}", "hyb": "hyb_in", "swa": "swa_in"}[kind]]
                mixed = n > 0 and stages[n - 1][0] != "ffn"
                if n == 1:
                    act_e.wait_ge(vec_ready, 2)
                if kind == "hyb":
                    act_e.wait_ge(rest_loaded, 16 * 5)
                    nc.scalar.activation(wba_hi, wba_pad, ACT.Copy).then_inc(wba_hi_ready, 1)
                if n == 0:
                    norm_scalar(act_e, n, lambda j: j >= 2 and first_split(act_e, j - 2))
                    split_hi(act_e, (1, 0), check=False)
                    split_hi(act_e, (2, 0), check=False)
                    load_rest(act_e)
                else:
                    norm_scalar(act_e, n, (lambda j: j < 2 and split_hi(act_e, (c - 1 + j, 0))) if mixed else None)
                    if mixed:
                        split_hi(act_e, (c + 1, 0))
                    split_hi(act_e, (c + 2, 0))
                norm_rstd(act_e, n)
                if kind == "ffn":
                    ffn_scalar(act_e, f, n)
                elif kind == "hyb":
                    hyb_scalar(act_e, n)
                else:
                    swa_scalar(act_e, n)
            for b in range(TB):
                for half in range(2):
                    k = 2 * b + half
                    if k < 2 * TB - 1:
                        act_e.wait_ge(fin_acc, k + 1)
                    else:
                        act_e.wait_ge(w_used, CHUNKS)
                    nc.scalar.activation(fin_t[:, k * 512:(k + 1) * 512], ACC[k][:], ACT.Square,
                                         accum_out=fin_ss[:, b, half:half + 1]).then_inc(fin_sq, 1)

        @block.vector
        def _(dve):
            dve.wait_ge(vec_turned, 1)
            nc.vector.tensor_copy(vecT[:, 0:FIRST_VEC], AUX[:, 0:FIRST_VEC]).then_inc(vec_ready, 1)
            dve.wait_ge(vec_ready, 1)
            for n, (kind, f) in enumerate(stages):
                c = first[{"ffn": f"ffn{f}", "hyb": "hyb_in", "swa": "swa_in"}[kind]]
                mixed = n > 0 and stages[n - 1][0] != "ffn"
                banks, ready = update(n)
                if n == 1:
                    dve.wait_ge(vec_ready, 2)
                norm_vector(dve, n, banks, ready,
                            vecT[:, V_BO:V_BO + KT] if n and stages[n - 1][0] == "swa" else None,
                            (c - 1, 0) if mixed else None)
                if n == 0:
                    split_lo(dve, (c, 0))
                split_lo(dve, (c + 1, 0), handed_over=mixed)
                norm_var(dve, n)
                split_lo(dve, (c + 2, 0))
                dve.wait_ge(rstd_ready, n + 1)
                if kind == "ffn":
                    ffn_vector(dve, f, n)
                elif kind == "hyb":
                    hyb_vector(dve, n)
                else:
                    swa_vector(dve, n)
            dve.wait_ge(final_loaded, 16)
            for b in range(TB):
                dve.wait_ge(fin_sq, 2 * b + 2)
                nc.vector.tensor_tensor(fin_v[:, b:b + 1], fin_ss[:, b, 0:1], fin_ss[:, b, 1:2], ALU.add) \
                  .then_inc(fin_sum, 1)
                dve.wait_ge(fin_sum, b + 1)
                nc.vector.tensor_scalar(fin_v[:, b:b + 1], fin_v[:, b:b + 1], 1.0 / D, EPS, ALU.mult, ALU.add) \
                  .then_inc(fin_var, 1)
                dve.wait_ge(fin_rstd, b + 1)
                for half in range(2):
                    cols = slice(half * 512, (half + 1) * 512)
                    nc.vector.scalar_tensor_tensor(out=y_out[:, b, cols], in0=ACC[2 * b + half][:],
                                                   scalar=fin_r[:, b:b + 1], in1=final_g[:, cols],
                                                   op0=ALU.mult, op1=ALU.mult).then_inc(out_ready, 1)

        @block.tensor
        def _(pe):
            pe.wait_ge(ident_loaded, 16)
            pe.wait_ge(first_vec_loaded, 16)
            nc.tensor.transpose(AUX[:, 0:FIRST_VEC], vec_rows[0:FIRST_VEC, :], ident[0:FIRST_VEC, 0:FIRST_VEC]) \
              .then_inc(vec_turned, 1)
            pe.wait_ge(x_loaded, 16)
            for j in range(PAIRS):
                if j == PAIRS // 2:
                    pe.wait_ge(x_loaded2, 16)
                for kt in (2 * j, 2 * j + 1):
                    for b in range(TB):
                        o = (kt % 2) * SEQ + b * P
                        last = nc.tensor.transpose(ACC[j][:, o:o + P], x_in[:, b, kt * P:(kt + 1) * P], ident)
                last.then_inc(acc_done, 1)
            for n, (kind, f) in enumerate(stages):
                if n == 0:
                    pe.wait_ge(vec_ready, 1)
                    pe.wait_ge(set_up, 2)
                if kind == "ffn":
                    ffn_tensor(pe, f, n)
                elif kind == "hyb":
                    hyb_tensor(pe, n)
                else:
                    swa_tensor(pe, n)


_INS = ["x", "ffn1_norm", "ffn1_w_gate", "ffn1_w_up", "ffn1_w_down", "mix_norm", "ffn2_norm", "ffn2_w_gate",
        "ffn2_w_up", "ffn2_w_down", "hyb_w_in", "gdn_conv_w", "gdn_a_log", "gdn_dt_bias", "gdn_out_norm",
        "sc_conv_w", "hyb_w_out", "swa_w_qkv", "swa_b_qkv", "swa_sinks", "swa_w_o", "swa_b_o", "final_norm"]


def build(nc, arrays):
    t = {}
    for name, a in arrays.items():
        t[name] = nc.dram_tensor(f"in_{name}", a.shape, F32, kind="ExternalInput").ap()
    out = nc.dram_tensor("out", (256, 1024), F32, kind="ExternalOutput").ap()
    trunk(nc, t, out)


def kernel(**inputs):
    import numpy as _np
    import concourse.bacc as _bacc
    from concourse.bass_utils import run_bass_kernel_spmd as _run

    nc = _bacc.Bacc("TRN2", target_bir_lowering=False, num_devices=1)
    arrays = {name: _np.ascontiguousarray(inputs[name]) for name in _INS}
    arrays["constants"] = constants()
    build(nc, arrays)
    r = _run(nc, [{f"in_{k}": v for k, v in arrays.items()}], core_ids=[0])
    return r.results[0]["out"].reshape(1, 256, 1024)
```
